# Optimizing a Trainium2 kernel written in Bass

```python
import math
import jax
import jax.numpy as jnp
from jax import lax
import numpy as np

D_MODEL = 1024
BATCH = 1
SEQ = 128
DEPTH = 2
DEC_BATCH = 1
DEC_SEQ = 512
PAST_LEN = 128

GRID_W = 64
CONV_W = 256
CONV_K = 31
NA_HEADS = 4
NA_HEAD_DIM = 64
NA_W = NA_HEADS * NA_HEAD_DIM
NA_ROWS_MAX = 8
NA_COLS = 16
NA_QB = 16
NA_KB = NA_QB + NA_COLS
NA_CTX_QB = 128
DN_HEADS = 4
DN_DK = 128
DN_DV = 128
DN_QK_W = DN_HEADS * DN_DK
DN_V_W = DN_HEADS * DN_DV
DN_CONV_K = 5
DN_CHUNK = 64
ROPE_BASE = 10000.0
MIX_W = CONV_W + NA_W + DN_V_W
OFF_CONV = 0
OFF_NA = OFF_CONV + 2 * CONV_W
OFF_DN_QKV = OFF_NA + 3 * NA_W
OFF_DN_Z = OFF_DN_QKV + 2 * DN_QK_W + DN_V_W
OFF_DN_AB = OFF_DN_Z + DN_V_W
PROJ_W = OFF_DN_AB + 4 * DN_HEADS
N_GROUPS = 4
EXPERTS_PER_GROUP = 4
N_EXPERTS = N_GROUPS * EXPERTS_PER_GROUP
TOP_K = 2
D_EXPERT = 256
EPS = 1e-6
NEG_INF = -1e30

kernel_name = "hybrid_conv_natten_deltanet_hmoe_prefix_step"

def rmsnorm(x, g):
    xf = x.astype(jnp.float32)
    y = xf * lax.rsqrt(jnp.mean(xf * xf, axis=-1, keepdims=True) + EPS)
    return (y * g.astype(jnp.float32)).astype(x.dtype)

def layernorm(x, g, b):
    xf = x.astype(jnp.float32)
    mu = jnp.mean(xf, axis=-1, keepdims=True)
    xc = xf - mu
    var = jnp.mean(xc * xc, axis=-1, keepdims=True)
    return (xc * lax.rsqrt(var + EPS) * g.astype(jnp.float32) + b.astype(jnp.float32)).astype(x.dtype)

def l2norm(x):
    return x * lax.rsqrt(jnp.sum(x * x, axis=-1, keepdims=True) + EPS)

def depthwise_conv(x, w):
    pad = (w.shape[0] - 1) // 2
    return lax.conv_general_dilated(x, w[:, None, :].astype(x.dtype), (1,), [(pad, pad)],
                                    dimension_numbers=('NWC', 'WIO', 'NWC'),
                                    feature_group_count=x.shape[-1])

def adaln(cond, w_mod, b_mod):
    m = jax.nn.silu(cond) @ w_mod + b_mod
    return jnp.split(m[:, None, :], 6, axis=-1)

def modulated_norm(x, g, shift, scale):
    return rmsnorm(x, g) * (1 + scale) + shift

def split_projection(p):
    b, t, _ = p.shape
    glu = p[..., OFF_CONV:OFF_NA]
    na = p[..., OFF_NA:OFF_DN_QKV].reshape(b, t, 3, NA_HEADS, NA_HEAD_DIM)
    return (glu, na[:, :, 0], na[:, :, 1], na[:, :, 2],
            p[..., OFF_DN_QKV:OFF_DN_Z], p[..., OFF_DN_Z:OFF_DN_AB], p[..., OFF_DN_AB:PROJ_W])

def conformer_conv(glu, conv_w, conv_b, ln_g, ln_b):
    u = glu[..., :CONV_W] * jax.nn.sigmoid(glu[..., CONV_W:])
    u = depthwise_conv(u, conv_w) + conv_b
    return jax.nn.silu(layernorm(u, ln_g, ln_b))

def context_attention(q, k, v):
    b, s, h, d = q.shape
    qb = (q * d ** -0.5).reshape(b, s // NA_CTX_QB, NA_CTX_QB, h, d).transpose(1, 0, 2, 3, 4)

    def one_block(qblk):
        sc = jnp.einsum('bqhd,bkhd->bhqk', qblk, k).astype(jnp.float32)
        pr = jax.nn.softmax(sc, axis=-1).astype(v.dtype)
        return jnp.einsum('bhqk,bkhd->bqhd', pr, v)

    o = lax.map(one_block, qb)
    return o.transpose(1, 0, 2, 3, 4).reshape(b, s, h * d)

def na_indices(rows):
    kr = min(NA_ROWS_MAX, rows)
    r = np.arange(rows)
    rs = np.clip(r - kr // 2, 0, rows - kr)
    row_idx = rs[:, None] + np.arange(kr)[None, :]
    row_off = row_idx - r[:, None] + NA_ROWS_MAX - 1
    n_cb = GRID_W // NA_QB
    j = np.arange(n_cb)
    kc0 = np.clip(j * NA_QB - NA_COLS // 2, 0, GRID_W - NA_KB)
    col_idx = kc0[:, None] + np.arange(NA_KB)[None, :]
    qcol = j[:, None] * NA_QB + np.arange(NA_QB)[None, :]
    cs = np.clip(qcol - NA_COLS // 2, 0, GRID_W - NA_COLS)[..., None]
    kcol = col_idx[:, None, :]
    col_mask = (kcol >= cs) & (kcol < cs + NA_COLS)
    col_off = np.clip(kcol - qcol[..., None] + NA_COLS - 1, 0, 2 * NA_COLS - 2)
    return kr, row_idx, row_off, col_idx, col_mask, col_off

def neighbourhood_attention(q, k, v, k_ctx, v_ctx, rel_bias):
    b, t, h, d = q.shape
    rows = t // GRID_W
    n_cb = GRID_W // NA_QB
    s_ctx_len = k_ctx.shape[1]
    kr, row_idx, row_off, col_idx, col_mask, col_off = na_indices(rows)
    q = q * d ** -0.5
    qb = q.reshape(b, rows, n_cb, NA_QB, h, d)
    kg = k.reshape(b, rows, GRID_W, h, d)
    vg = v.reshape(b, rows, GRID_W, h, d)
    ri = jnp.asarray(row_idx)[:, :, None, None]
    ci = jnp.asarray(col_idx)[None, None, :, :]
    kb = kg[:, ri, ci]
    vb = vg[:, ri, ci]
    s_loc = jnp.einsum('brjqhd,brkjchd->bhrjqkc', qb, kb).astype(jnp.float32)
    bias = rel_bias[:, jnp.asarray(row_off)[:, None, None, :, None],
                    jnp.asarray(col_off)[None, :, :, None, :]]
    s_loc = s_loc + bias[None].astype(jnp.float32)
    s_loc = jnp.where(jnp.asarray(col_mask)[None, None, None, :, :, None, :], s_loc, NEG_INF)
    s_loc = s_loc.reshape(b, h, rows, n_cb, NA_QB, kr * NA_KB)
    s_ctx = jnp.einsum('bthd,bshd->bhts', q, k_ctx).astype(jnp.float32)
    s_ctx = s_ctx.reshape(b, h, rows, n_cb, NA_QB, s_ctx_len)
    pr = jax.nn.softmax(jnp.concatenate([s_loc, s_ctx], axis=-1), axis=-1)
    p_loc = pr[..., :kr * NA_KB].reshape(b, h, rows, n_cb, NA_QB, kr, NA_KB).astype(v.dtype)
    p_ctx = pr[..., kr * NA_KB:].reshape(b, h, t, s_ctx_len).astype(v.dtype)
    o_loc = jnp.einsum('bhrjqkc,brkjchd->brjqhd', p_loc, vb).reshape(b, t, h * d)
    o_ctx = jnp.einsum('bhts,bshd->bthd', p_ctx, v_ctx).reshape(b, t, h * d)
    return o_loc + o_ctx

def axial_rope_tables(t):
    pos = np.arange(t)
    n_freq = DN_DK // 4
    inv = ROPE_BASE ** (-np.arange(n_freq) / n_freq)
    ang = np.stack([(pos // GRID_W)[:, None] * inv[None, :],
                    (pos % GRID_W)[:, None] * inv[None, :]], axis=1)
    return jnp.asarray(np.cos(ang), dtype=jnp.float32), jnp.asarray(np.sin(ang), dtype=jnp.float32)

def apply_axial_rope(x, cos, sin):
    b, t, h, d = x.shape
    xr = x.reshape(b, t, h, 2, 2, d // 4)
    x1, x2 = xr[..., 0, :], xr[..., 1, :]
    cs, sn = cos[None, :, None], sin[None, :, None]
    return jnp.stack([x1 * cs - x2 * sn, x2 * cs + x1 * sn], axis=-2).reshape(b, t, h, d)

def chunk_gated_delta(q, k, v, g, beta, s0):
    b, t, h, dk = q.shape
    dv = v.shape[-1]
    n = t // DN_CHUNK

    def blk(a):
        return jnp.moveaxis(a.reshape(b, n, DN_CHUNK, h, -1), 3, 1)

    q, k, v = blk(q), blk(k), blk(v)
    gc = jnp.cumsum(blk(g[..., None])[..., 0], axis=-1)
    be = blk(beta[..., None])[..., 0]
    tri = jnp.tril(jnp.ones((DN_CHUNK, DN_CHUNK), dtype=bool))
    strict = jnp.tril(jnp.ones((DN_CHUNK, DN_CHUNK), dtype=bool), -1)
    diff = gc[..., :, None] - gc[..., None, :]
    decay = jnp.where(tri, jnp.exp(jnp.where(tri, diff, 0.0)), 0.0)
    kb = k * be[..., None]
    a_mat = jnp.where(strict, jnp.einsum('bhnid,bhnjd->bhnij', kb, k) * decay, 0.0)
    rhs = jnp.concatenate([v * be[..., None], kb * jnp.exp(gc)[..., None]], axis=-1)
    sol = lax.linalg.triangular_solve(a_mat + jnp.eye(DN_CHUNK, dtype=a_mat.dtype), rhs,
                                      left_side=True, lower=True, unit_diagonal=True)
    u_base, w_dec = sol[..., :dv], sol[..., dv:]
    a_qk = jnp.einsum('bhnid,bhnjd->bhnij', q, k) * decay
    q_dec = q * jnp.exp(gc)[..., None]
    k_dec = k * jnp.exp(gc[..., -1:] - gc)[..., None]
    c_dec = jnp.exp(gc[..., -1])

    def step(s, inp):
        ub, wd, aqk, qd, kd, cd = inp
        u = ub - jnp.einsum('bhcd,bhde->bhce', wd, s)
        o = jnp.einsum('bhcd,bhde->bhce', qd, s) + jnp.einsum('bhij,bhje->bhie', aqk, u)
        s = s * cd[..., None, None] + jnp.einsum('bhcd,bhce->bhde', kd, u)
        return s, o

    mv = lambda a: jnp.moveaxis(a, 2, 0)
    s_fin, o = lax.scan(step, s0, (mv(u_base), mv(w_dec), mv(a_qk), mv(q_dec), mv(k_dec), mv(c_dec)))
    o = o.transpose(1, 0, 3, 2, 4).reshape(b, t, h, dv)
    return o, s_fin

def gated_deltanet(dn_qkv, dn_z, dn_ab, conv_w, a_log, dt_bias, norm_g, s_fwd, s_bwd, rope):
    b, t, _ = dn_qkv.shape
    qkv = jax.nn.silu(depthwise_conv(dn_qkv, conv_w)).astype(jnp.float32)
    q = l2norm(qkv[..., :DN_QK_W].reshape(b, t, DN_HEADS, DN_DK))
    k = l2norm(qkv[..., DN_QK_W:2 * DN_QK_W].reshape(b, t, DN_HEADS, DN_DK))
    v = qkv[..., 2 * DN_QK_W:].reshape(b, t, DN_HEADS, DN_DV)
    if rope is not None:
        q = apply_axial_rope(q, rope[0], rope[1])
        k = apply_axial_rope(k, rope[0], rope[1])
    q = q * DN_DK ** -0.5
    ab = dn_ab.astype(jnp.float32).reshape(b, t, 4, DN_HEADS)
    g = -jnp.exp(a_log.astype(jnp.float32)) * jax.nn.softplus(ab[:, :, 0:2] + dt_bias.astype(jnp.float32))
    beta = jax.nn.sigmoid(ab[:, :, 2:4])
    o_f, s_f = chunk_gated_delta(q, k, v, g[:, :, 0], beta[:, :, 0], s_fwd.astype(jnp.float32))
    fl = lambda a: jnp.flip(a, axis=1)
    o_b, s_b = chunk_gated_delta(fl(q), fl(k), fl(v), fl(g[:, :, 1]), fl(beta[:, :, 1]),
                                 s_bwd.astype(jnp.float32))
    o = rmsnorm(o_f + fl(o_b), norm_g) * jax.nn.silu(dn_z.astype(jnp.float32).reshape(b, t, DN_HEADS, DN_DV))
    return o.reshape(b, t, DN_V_W).astype(dn_qkv.dtype), jnp.stack([s_f, s_b], axis=1)

def hierarchical_moe(h, wg, bg, we, be, w1, w3, w2):
    b, t, d = h.shape
    x = h.reshape(b * t, d)
    pg = jax.nn.softmax((x @ wg).astype(jnp.float32) + bg.astype(jnp.float32), axis=-1)
    pg_sel, g_sel = lax.top_k(pg, 1)
    le = ((x @ we).astype(jnp.float32) + be.astype(jnp.float32)).reshape(-1, N_GROUPS, EXPERTS_PER_GROUP)
    le_sel = jnp.take_along_axis(le, g_sel[:, :, None], axis=1)[:, 0]
    w_top, i_top = lax.top_k(jax.nn.softmax(le_sel, axis=-1), TOP_K)
    w_top = w_top / jnp.sum(w_top, axis=-1, keepdims=True) * pg_sel
    e_idx = g_sel * EXPERTS_PER_GROUP + i_top
    gates = jnp.sum(jax.nn.one_hot(e_idx, N_EXPERTS, dtype=jnp.float32) * w_top[..., None], axis=1)
    hid = jax.nn.silu(jnp.einsum('nd,edf->nef', x, w1)) * jnp.einsum('nd,edf->nef', x, w3)
    y = jnp.einsum('nef,efd->nd', hid * gates[:, :, None].astype(hid.dtype), w2)
    return y.reshape(b, t, d)

def setup_inputs(seed: int = 0) -> dict:
    key = jax.random.key(seed)
    ks = jax.random.split(key, 32)
    nrm = lambda k, shape, s: jax.random.normal(k, shape, jnp.float32) * s
    L, D = DEPTH, D_MODEL
    dt = jnp.exp(jax.random.uniform(ks[19], (L, 2, DN_HEADS), jnp.float32, math.log(1e-3), math.log(0.1)))
    return {
        'x_prompt': nrm(ks[0], (BATCH, SEQ, D), 1.0),
        'x_sample': nrm(ks[1], (DEC_BATCH, DEC_SEQ, D), 1.0),
        'cache_na_k': nrm(ks[2], (DEC_BATCH, L, PAST_LEN, NA_HEADS, NA_HEAD_DIM), 1.0),
        'cache_na_v': nrm(ks[3], (DEC_BATCH, L, PAST_LEN, NA_HEADS, NA_HEAD_DIM), 1.0),
        'state_delta': nrm(ks[4], (DEC_BATCH, L, 2, DN_HEADS, DN_DK, DN_DV), 0.1),
        'c': nrm(ks[5], (DEC_BATCH, D), 1.0),
        'c_ctx': nrm(ks[6], (D,), 1.0),
        'w_mod': nrm(ks[7], (L, D, 6 * D), 0.5 * D ** -0.5),
        'b_mod': nrm(ks[8], (L, 6 * D), 0.01),
        'g_norm1': 1.0 + nrm(ks[9], (L, D), 0.01),
        'g_norm2': 1.0 + nrm(ks[10], (L, D), 0.01),
        'w_in': nrm(ks[11], (L, D, PROJ_W), D ** -0.5),
        'conv_a_w': nrm(ks[12], (L, CONV_K, CONV_W), CONV_K ** -0.5),
        'conv_a_b': nrm(ks[13], (L, CONV_W), 0.01),
        'ln_a_g': 1.0 + nrm(ks[14], (L, CONV_W), 0.01),
        'ln_a_b': nrm(ks[15], (L, CONV_W), 0.01),
        'na_rel_bias': nrm(ks[16], (L, NA_HEADS, 2 * NA_ROWS_MAX - 1, 2 * NA_COLS - 1), 0.2),
        'dn_conv_w': nrm(ks[17], (L, DN_CONV_K, 2 * DN_QK_W + DN_V_W), DN_CONV_K ** -0.5),
        'dn_a_log': jnp.log(jax.random.uniform(ks[18], (L, 2, DN_HEADS), jnp.float32, 1.0, 16.0)),
        'dn_dt_bias': dt + jnp.log(-jnp.expm1(-dt)),
        'dn_norm_g': 1.0 + nrm(ks[20], (L, DN_DV), 0.01),
        'w_out': nrm(ks[21], (L, MIX_W, D), MIX_W ** -0.5),
        'router_wg': nrm(ks[22], (L, D, N_GROUPS), D ** -0.5),
        'router_bg': nrm(ks[23], (L, N_GROUPS), 0.01),
        'router_we': nrm(ks[24], (L, D, N_EXPERTS), D ** -0.5),
        'router_be': nrm(ks[25], (L, N_EXPERTS), 0.01),
        'w1': nrm(ks[26], (L, N_EXPERTS, D, D_EXPERT), D ** -0.5),
        'w3': nrm(ks[27], (L, N_EXPERTS, D, D_EXPERT), D ** -0.5),
        'w2': nrm(ks[28], (L, N_EXPERTS, D_EXPERT, D), D_EXPERT ** -0.5),
        'g_final': 1.0 + nrm(ks[29], (D,), 0.01),
    }

def reference(x_prompt, x_sample, cache_na_k, cache_na_v, state_delta, c, c_ctx, w_mod, b_mod,
              g_norm1, g_norm2, w_in, conv_a_w, conv_a_b, ln_a_g, ln_a_b, na_rel_bias, dn_conv_w,
              dn_a_log, dn_dt_bias, dn_norm_g, w_out, router_wg, router_bg, router_we, router_be,
              w1, w3, w2, g_final):
    xc = x_prompt
    new_k, new_v, new_s = [], [], []
    for l in range(DEPTH):
        sh1, sc1, ga1, sh2, sc2, ga2 = adaln(c_ctx[None, :], w_mod[l], b_mod[l])
        p = modulated_norm(xc, g_norm1[l], sh1, sc1) @ w_in[l]
        glu, q_na, k_na, v_na, dn_qkv, dn_z, dn_ab = split_projection(p)
        out_a = conformer_conv(glu, conv_a_w[l], conv_a_b[l], ln_a_g[l], ln_a_b[l])
        out_b = context_attention(q_na, k_na, v_na)
        s0 = jnp.zeros((xc.shape[0], DN_HEADS, DN_DK, DN_DV), jnp.float32)
        out_c, s_ctx = gated_deltanet(dn_qkv, dn_z, dn_ab, dn_conv_w[l], dn_a_log[l], dn_dt_bias[l],
                                      dn_norm_g[l], s0, s0, None)
        xc = xc + ga1 * (jnp.concatenate([out_a, out_b, out_c], axis=-1) @ w_out[l])
        xc = xc + ga2 * hierarchical_moe(modulated_norm(xc, g_norm2[l], sh2, sc2), router_wg[l], router_bg[l],
                                         router_we[l], router_be[l], w1[l], w3[l], w2[l])
        new_k.append(k_na)
        new_v.append(v_na)
        new_s.append(s_ctx)
    y_prompt = rmsnorm(xc, g_final)
    new_cache_na_k = jnp.stack(new_k, axis=1)
    new_cache_na_v = jnp.stack(new_v, axis=1)
    new_state_delta = jnp.stack(new_s, axis=1)

    xs = x_sample
    rope = axial_rope_tables(xs.shape[1])
    for l in range(DEPTH):
        sh1, sc1, ga1, sh2, sc2, ga2 = adaln(c, w_mod[l], b_mod[l])
        p = modulated_norm(xs, g_norm1[l], sh1, sc1) @ w_in[l]
        glu, q_na, k_na, v_na, dn_qkv, dn_z, dn_ab = split_projection(p)
        out_a = conformer_conv(glu, conv_a_w[l], conv_a_b[l], ln_a_g[l], ln_a_b[l])
        out_b = neighbourhood_attention(q_na, k_na, v_na, cache_na_k[:, l], cache_na_v[:, l], na_rel_bias[l])
        out_c, _ = gated_deltanet(dn_qkv, dn_z, dn_ab, dn_conv_w[l], dn_a_log[l], dn_dt_bias[l],
                                  dn_norm_g[l], state_delta[:, l, 0], state_delta[:, l, 1], rope)
        xs = xs + ga1 * (jnp.concatenate([out_a, out_b, out_c], axis=-1) @ w_out[l])
        xs = xs + ga2 * hierarchical_moe(modulated_norm(xs, g_norm2[l], sh2, sc2), router_wg[l], router_bg[l],
                                         router_we[l], router_be[l], w1[l], w3[l], w2[l])
    y_sample = rmsnorm(xs, g_final)
    return (y_prompt, y_sample, new_cache_na_k, new_cache_na_v, new_state_delta)


_drawn_inputs = setup_inputs


def setup_inputs(seed=0):
    import zlib

    import numpy as np

    out = dict(_drawn_inputs(seed))
    spreads = {}
    factors = {'cache_na_k': 3.024,
     'cache_na_v': 2.678,
     'state_delta': 3.178,
     'g_norm1': 3.714,
     'g_norm2': 5.977,
     'conv_a_b': 8.0,
     'ln_a_g': 56.268,
     'ln_a_b': 8.0,
     'na_rel_bias': 7.176,
     'dn_norm_g': 8.0,
     'router_bg': 5.336,
     'router_be': 8.0,
     'g_final': 35.001}
    for name, (base, spread) in spreads.items():
        noise = np.random.default_rng([zlib.crc32(name.encode()), seed]).standard_normal(out[name].shape)
        drawn = base * np.exp(spread * noise) if base else spread * noise
        out[name] = jnp.asarray(drawn.astype(out[name].dtype))
    for name, factor in factors.items():
        out[name] = (out[name] * factor).astype(out[name].dtype)
    return out
```

```python
from contextlib import ExitStack

import numpy as np
import concourse.bass as bass
from concourse import mybir
from concourse.alu_op_type import AluOpType as ALU

ACT = mybir.ActivationFunctionType
F32 = mybir.dt.float32
AX = mybir.AxisListType.X

P = 128
L = 2
D = 1024
KD = D // P
TS, TC = 512, 128
T = TS + TC
NCH = T // P
GRID = 64
CW, CK = 256, 31
NAW, NH, HD = 256, 4, 64
DNW, DH, DK = 512, 4, 128
DCK = 5
OFF_AB = 2 * CW + 3 * NAW + 3 * DNW + DNW
PROJ = 2 * CW + 3 * NAW + 3 * DNW + DNW + 4 * DH
NE, NG, EPG, FE = 16, 4, 4, 256
FT = FE // P
EPS = 1e-6
NEG = -1e30
CPAD, DPAD = (CK - 1) // 2, (DCK - 1) // 2
CLEN = TS + CPAD + TC
DLEN = TS + DPAD + TC
DST = DLEN + 2
CU, SLEN = CLEN + 2 * CPAD, DLEN + 2 * DPAD
RO, CO = 15, 31
LEV = 7

IN_CHUNKS = [(0, 512), (1280, 512), (1792, 512), (2304, 512), (2816, 512), (512, 512), (1024, 256)]
SLOT = KD * 512
PRM_DMAS = 17
ACT_STEPS, DVE_STEPS, POOL_STEPS = 17, 202, 1

R_BMOD, R_G1, R_G2, R_CW, R_CB = 0, 48, 56, 64, 126
R_LNG, R_LNB, R_DW, R_NG, R_GF = 128, 130, 132, 192, 193
NROW2 = 201 - 128

G_GLU, G_DN, G_Z, G_QK = 0, 4, 16, 20
G_ATT, G_CTX, G_OUT, G_MOE = 24, 40, 42, 50
G_PAIR = 24
G_ALL = G_MOE + G_PAIR * NE // 2

C_ID, C_PERM, C_ONE = 0, 128, 256
C_COS, C_SIN = 384, 896
C_UP, C_LO = 1408, 1536
C_LEV = 1664
C_COL = C_LEV + 2 * LEV * P
C_NEG = C_COL + GRID
C_IOTA = C_NEG + GRID
C_SC = C_IOTA + 4
NC = C_SC + 4


def constants():
    c = np.zeros((P, NC), np.float32)
    i = np.arange(P)
    c[:, C_ID:C_ID + P] = np.eye(P)
    c[i, C_PERM + (i ^ 32)] = 1.0
    c[:, C_ONE:C_ONE + P] = 1.0
    pos = np.arange(TS)
    nf = DK // 4
    inv = 10000.0 ** (-np.arange(nf) / nf)
    for d in range(P):
        ang = (pos // GRID if d < 64 else pos % GRID) * inv[d % 32]
        c[d, C_COS:C_COS + TS] = np.cos(ang)
        c[d, C_SIN:C_SIN + TS] = np.sin(ang) * (-1.0 if d % 64 < 32 else 1.0)
    a, b = i[:, None], i[None, :]
    c[:, C_UP:C_UP + P] = a <= b
    c[:, C_LO:C_LO + P] = a >= b
    for n in range(LEV):
        s = 1 << n
        fw = (a // (2 * s) == b // (2 * s)) & (b // s == a // s + 1)
        c[:, C_LEV + n * P:C_LEV + (n + 1) * P] = fw
        c[:, C_LEV + (LEV + n) * P:C_LEV + (LEV + n + 1) * P] = fw.T
    q, k = (i % GRID)[:, None], np.arange(GRID)[None, :]
    cs = np.clip(q - 8, 0, GRID - 16)
    c[:, C_COL:C_COL + GRID] = (k >= cs) & (k < cs + 16)
    c[:, C_NEG:C_NEG + GRID] = NEG * (1.0 - c[:, C_COL:C_COL + GRID])
    c[:, C_IOTA:C_IOTA + 4] = np.arange(4)
    c[:, C_SC] = EPS
    c[:, C_SC + 1] = -0.5 * np.log(DK)
    c[:, C_SC + 2] = 1.0
    return c


class Signal:

    def __init__(self, sem, per_layer, first=0):
        self.sem, self.per_layer, self.first = sem, per_layer, first

    def at(self, layer, n):
        return layer * self.per_layer + (n + self.first)


def build(nc, x_prompt, x_sample, cache_k, cache_v, state, c, c_ctx, w_mod, b_mod, g1, g2, w_in, conv_w,
          conv_b, ln_g, ln_b, rel_bias, dn_conv_w, a_log, dt_bias, norm_g, w_out, wg, bg, we, be, w1, w3, w2,
          g_final, consts, y_prompt, y_sample, new_k, new_v, new_s, dbg=None):
    BP = GRID + NH * RO * CO + GRID
    bias_pad = nc.dram_tensor("bias_pad", (GRID, BP), F32, kind="Internal")
    gate_rows = nc.dram_tensor("gate_rows", (NE, T), F32, kind="Internal").ap()
    NB = NH * RO * CO

    with ExitStack() as ctx:
        def sb(name, shape):
            return ctx.enter_context(nc.sbuf_tensor(name, shape, F32))

        def signal(name, per_layer, first=0):
            return Signal(ctx.enter_context(nc.semaphore(name)), per_layer, first)

        def heads(ap):
            return ap.rearrange("p (h n) -> p h n", h=4)

        ps = ctx.enter_context(nc.psum_tensor("ps", [P, 8 * 512], F32))
        ring = [sb(f"ring{i}", [P, SLOT]) for i in range(3)]
        xT = sb("xT", [P, KD, T])
        hreg = sb("hreg", [P, KD * T])
        hT = hreg[:, :].rearrange("p (k t) -> p k t", k=KD)
        dnT = sb("dnT", [P, 12, DST])
        tok = sb("tok", [P, 2, NCH, DH * DK])
        zs = sb("zs", [P, DH, T])
        mixA = sb("mixA", [P, 2, CLEN])
        mixb_reg = sb("mixb_reg", [P, 2 * SLEN])
        mixB = mixb_reg[:, 0:2 * T].rearrange("p (t n) -> p t n", t=2)
        stage = [mixb_reg[:, SLEN * i:SLEN * (i + 1)] for i in range(2)]
        cst = sb("cst", [P, NC])
        work = sb("work", [P, 6 * T])
        small = sb("small", [P, 1110])
        rst = sb("rst", [P, T])[:, :]
        tmp_reg = sb("tmp_reg", [P, 2 * CLEN])
        tmp = tmp_reg[:, :].rearrange("p (t n) -> p t n", t=2)
        prm = tmp_reg[:, 0:2 * P].rearrange("p (t n) -> p t n", t=2)
        cin_reg = sb("cin_reg", [P, 2 * CU])
        cin = cin_reg[:, :].rearrange("p (t n) -> p t n", t=2)
        S = [heads(cin_reg[:, 512 * d:512 * d + 512]) for d in range(2)]
        qkT = work[:, 0:4 * T].rearrange("p (t n) -> p t n", t=4)
        vna = work[:, 4 * T:4 * T + NCH * NAW].rearrange("p (t n) -> p t n", t=NCH)
        at = [0]

        def carve(n):
            at[0] += n
            return small[:, at[0] - n:at[0]]

        pT = carve(201)
        condT = carve(2 * KD)
        mod = carve(96).rearrange("p (j c) -> p j c", c=2)
        A = [carve(2 * KD).rearrange("p (j c) -> p j c", c=2) for _ in range(2)]
        alog, dtb, ealog = carve(8), carve(8), carve(8)
        rbias = carve(20)
        wr = carve(KD * 20).rearrange("p (k n) -> p k n", k=KD)
        wab = carve(KD * 16).rearrange("p (k n) -> p k n", k=KD)
        st = carve(16)
        rt = small[:, at[0]:at[0] + 400]
        ab = carve(80).rearrange("p (c n) -> p c n", c=NCH)
        gsp = carve(40).rearrange("p (c n) -> p c n", c=NCH)
        gt1 = carve(40).rearrange("p (c n) -> p c n", c=NCH)
        beta = carve(40).rearrange("p (c n) -> p c n", c=NCH)
        gcum = carve(80)
        egc = carve(40)
        ekd = carve(40)
        cdec = carve(40)

        def gslot(s):
            return ps[:, 1024 * s:1024 * s + T]

        def bank(b, n=512):
            return ps[:, 512 * b:512 * b + n]

        ident = cst[:, C_ID:C_ID + P]
        ones = cst[:, C_ONE:C_ONE + P]
        eps_c, lnsc_c, one_c = (cst[:, C_SC + i:C_SC + i + 1] for i in range(3))

        def over_heads(ap):
            return ap.rearrange("p (a n) -> p a n", a=1).to_broadcast([P, 4, ap.shape[-1]])

        def along(ap, n):
            return ap.rearrange("p (h a) -> p h a", a=1).to_broadcast([P, ap.shape[-1], n])

        names = ["DT", "CT", "aqk", "Cs0", "X", "XT", "W", "qdec", "kdec"]
        places = [[hreg[:, 512 * i:512 * i + 512] for i in range(9)],
                  [work[:, 512 * i:512 * i + 512] for i in range(7)] + [tmp_reg[:, 0:512], tmp_reg[:, 512:1024]]]
        B = [{n: heads(r) for n, r in zip(names, regs)} for regs in places]
        for b_ in B:
            b_["Cs1"] = b_["DT"]
        sc = [hreg[:, 640 * i:640 * i + 640] for i in range(2)]
        pT_ = [hreg[:, 640 * (2 + i):640 * (3 + i)] for i in range(2)]
        kvc = [hreg[:, 2560 + 256 * i:2816 + 256 * i] for i in range(2)]
        kcT = hreg[:, 3072:3328]
        newk = hreg[:, 3328:3584]
        rcos = [hreg[:, 3584 + 512 * i:4096 + 512 * i] for i in range(2)]
        rsin = hreg[:, 4608:5120]
        Tz = tok[:, :, :, :].rearrange("p a c n -> p (a c n)")[:, 0:NH * RO * GRID]
        tzv = Tz.rearrange("p (a n) -> p a n", n=GRID)
        hid = [dnT[:, i, 0:T] for i in range(4)]
        sil = [dnT[:, 4 + i, 0:T] for i in range(2)]
        gate = [dnT[:, 6 + i, 0:T] for i in range(2)]
        mb = [dnT[:, 8 + i, 0:T] for i in range(2)]
        gT = dnT[0:NE, 10, 0:T]
        xload = hreg[:, :].rearrange("p (c d) -> p c d", c=NCH)

        once = {n: ctx.enter_context(nc.semaphore(n)) for n in
                ("first_loaded", "x_turned", "cond_ready", "pad_ready", "pads_written", "cst_loaded", "y_turned", "y_copied",
                 "y_stored", "cond_turned", "fin_sq", "fin_ss", "fin_r", "fin_y", "pe_first")}
        ring_loaded = [signal(f"ring_loaded{i}", 16 * (7 + 16)) for i in range(2)] + [signal("ring_loaded2", 16 * 7)]
        w2_loaded = [signal(f"w2_loaded{i}", 16 * 8) for i in range(2)]
        mod_used = [signal(f"mod_used{i}", 4) for i in range(3)]
        gemm_done = signal("gemm_done", G_ALL, 1)
        gemm_out = [signal(f"gemm_out{i}", G_ALL // 2, 1) for i in range(2)]
        prm_loaded = signal("prm_loaded", 16 * PRM_DMAS)
        bias_copied = signal("bias_copied", 16)
        bias_loaded = signal("bias_loaded", 32)
        kvc_loaded = signal("kvc_loaded", 32)
        state_loaded = signal("state_loaded", 32)
        prm_turned = signal("prm_turned", 1)
        pT_ready = signal("pT_ready", 1)
        mod_ready = signal("mod_ready", 1)
        sq_ready = signal("sq_ready", 2 * KD)
        norm_ss = signal("norm_ss", 2)
        norm_r = signal("norm_r", 2)
        norm_x = signal("norm_x", 2 * KD)
        h_ready = signal("h_ready", 2 * KD)
        dn_conv = signal("dn_conv", 12)
        dn_silu = signal("dn_silu", 12)
        ab_done = signal("ab_done", 1)
        ab_copied = signal("ab_copied", 1)
        v_done = signal("v_done", 1)
        v_copied = signal("v_copied", 1)
        conv_out = signal("conv_out", 1)
        ln_sum = signal("ln_sum", 1)
        ln_xc = signal("ln_xc", 2)
        ln_sq = signal("ln_sq", 2)
        ln_var = signal("ln_var", 1)
        ln_r = signal("ln_r", 1)
        ln_y = signal("ln_y", 2)
        mixa_ready = signal("mixa_ready", 2)
        kc_turned = signal("kc_turned", 1)
        kc_copied = signal("kc_copied", 1)
        newk_turned = signal("newk_turned", 1)
        newk_copied = signal("newk_copied", 1)
        newkv_stored = signal("newkv_stored", 32)
        tz_ready = signal("tz_ready", 1)
        att_s = signal("att_s", 18)
        att_p = signal("att_p", 18)
        att_n = signal("att_n", 18)
        att_pt = signal("att_pt", 18)
        att_ptc = signal("att_ptc", 18)
        att_o = signal("att_o", 20)
        att_oc = signal("att_oc", 20)
        l2_sq = signal("l2_sq", 8)
        l2_ss = signal("l2_ss", 8)
        l2_r = signal("l2_r", 8)
        l2_x = signal("l2_x", 8)
        rope_mm = signal("rope_mm", 8)
        rope_cos = signal("rope_cos", 8)
        rope_x = signal("rope_x", 8)
        kv_turned = signal("kv_turned", 8)
        kv_copied = signal("kv_copied", 8)
        ctx_zero = signal("ctx_zero", 2)
        pads_zeroed = signal("pads_zeroed", 1)
        conv_in = signal("conv_in", 2)
        beta_tanh = signal("beta_tanh", 1)
        g_abs = signal("g_abs", 1)
        g_act = signal("g_act", 1)
        g_ready = signal("g_ready", 1)
        gc_done = signal("gc_done", 1)
        gc_copied = signal("gc_copied", 1)
        gc_exp = signal("gc_exp", 1)
        dn_row = signal("dn_row", 10)
        dn_gram = signal("dn_gram", 10)
        dn_erow = signal("dn_erow", 10)
        dn_dlog = signal("dn_dlog", 10)
        dn_dexp = signal("dn_dexp", 10)
        dn_mat = signal("dn_mat", 10)
        dn_cs = signal("dn_cs", 10 * LEV)
        dn_qk = signal("dn_qk", 20)
        dn_c1 = signal("dn_c1", 10)
        dn_x = signal("dn_x", 10 * LEV)
        dn_w = signal("dn_w", 10 * (LEV - 1))
        dn_wc = signal("dn_wc", 10 * (LEV - 1))
        dn_y = signal("dn_y", 10 * (LEV - 1))
        dn_ks = signal("dn_ks", 10)
        dn_res = signal("dn_res", 10)
        dn_u = signal("dn_u", 10)
        dn_uu = signal("dn_uu", 10)
        dn_o = signal("dn_o", 10)
        dn_state = signal("dn_state", 10)
        state_stored = signal("state_stored", 32)
        on_sq = signal("on_sq", 4)
        on_ss = signal("on_ss", 4)
        on_r = signal("on_r", 4)
        mixc_ready = signal("mixc_ready", 4)
        logits = signal("logits", 1)
        rt_in = signal("rt_in", 1)
        rt_exp = signal("rt_exp", 1)
        rt_in2 = signal("rt_in2", 1)
        rt_exp2 = signal("rt_exp2", 1)
        gates_ready = signal("gates_ready", 1)
        gates_turned = signal("gates_turned", 1)
        gates_copied = signal("gates_copied", 1)
        gates_stored = signal("gates_stored", 16)
        gate_loaded = [signal(f"gate_loaded{i}", 16 * 8) for i in range(2)]
        hid_ready = signal("hid_ready", 2 * NE, 2)
        act_step = signal("act_step", ACT_STEPS)
        dve_step = signal("dve_step", DVE_STEPS)
        pool_step = signal("pool_step", POOL_STEPS)

        block = ctx.enter_context(nc.Block())

        @block.sync
        def _(sp):
            sp.dma_start(cst[:, :], consts).then_inc(once["cst_loaded"], 16)
            sp.dma_start(xload[:, 0:4, :], x_sample[0].rearrange("(c p) d -> p c d", p=P)).then_inc(once["first_loaded"], 16)
            sp.dma_start(xload[:, 4, :], x_prompt[0]).then_inc(once["first_loaded"], 16)
            sp.dma_start(prm[0:8, 0, :], c[0].rearrange("(k p) -> k p", p=P)).then_inc(once["first_loaded"], 16)
            sp.dma_start(prm[8:16, 0, :], c_ctx.rearrange("(k p) -> k p", p=P)).then_inc(once["first_loaded"], 16)
            sp.wait_ge(once["pad_ready"], 1)
            for o in (0, GRID + NB):
                sp.dma_start(bias_pad.ap()[:, o:o + GRID], rst[0:GRID, 0:GRID]).then_inc(once["pads_written"], 16)
            with sp.Fori(0, L) as l:
                def need(sig, n):
                    sp.wait_ge(sig.sem, sig.at(l, n))

                for i in range(21):
                    s = i % 3
                    if i < 3:
                        need(gemm_done, 0)
                    elif i < 15:
                        need(mod_used[s], i // 3)
                    elif i - 15 < 4:
                        need(gemm_done, 4 * (i - 14))
                    elif i - 15 == 4:
                        need(gemm_done, G_Z + 4)
                    else:
                        need(gemm_done, G_QK + 4)
                    if i < 12:
                        src, w = w_mod[l][:, 512 * i:512 * i + 512], 512
                    elif i < 19:
                        o, w = IN_CHUNKS[i - 12]
                        src = w_in[l][:, o:o + w]
                    else:
                        src, w = w_out[l][:, 512 * (i - 19):512 * (i - 18)], 512
                    dst = ring[s][:, 0:KD * w].rearrange("p (k n) -> p k n", k=KD)
                    sp.dma_start(dst, src.rearrange("(k p) n -> p k n", p=P)).then_inc(ring_loaded[s].sem, 16)

                def expert_weights(pr, q):
                    e = pr * 2 + q
                    if not isinstance(pr, int):
                        sp.wait_ge(gemm_done.sem, gemm_done.at(l, G_MOE + 12 * q + 4 - G_PAIR) + pr * G_PAIR)
                    elif q == 0:
                        need(v_done, 1)
                    else:
                        need(gemm_done, G_OUT + 4)
                    for m, w in enumerate((w1, w3)):
                        dst = ring[q][:, 2048 * m:2048 * m + 2048].rearrange("p (k n) -> p k n", k=KD)
                        sp.dma_start(dst, w[l, e].rearrange("(k p) n -> p k n", p=P)).then_inc(ring_loaded[q].sem, 16)
                    if isinstance(pr, int):
                        need(gemm_done, G_OUT + 8)
                    else:
                        sp.wait_ge(gemm_done.sem, gemm_done.at(l, G_MOE + 12 * q + 12 - G_PAIR) + pr * G_PAIR)
                    dst = ring[2][:, 2048 * q:2048 * q + 2048].rearrange("p (k n) -> p k n", k=FT)
                    sp.dma_start(dst, w2[l, e].rearrange("(k p) n -> p k n", p=P)).then_inc(w2_loaded[q].sem, 16)
                    if isinstance(pr, int):
                        if q == 0:
                            need(gates_stored, 16)
                    else:
                        sp.wait_ge(hid_ready.sem, hid_ready.at(l, 2 * q - 2) + pr * 4)
                    sp.dma_start(gate[q], gate_rows[bass.ds(e, 1), :].to_broadcast([P, T])).then_inc(gate_loaded[q].sem, 16)

                expert_weights(0, 0)
                expert_weights(0, 1)
                with sp.Fori(1, NE // 2) as pr:
                    expert_weights(pr, 0)
                    expert_weights(pr, 1)
            sp.wait_ge(once["y_stored"], 32)

        @block.tensor
        def _(pe):
            mm = nc.tensor.matmul
            turn = nc.tensor.transpose

            pe.sem_inc(gemm_done.sem, 1)
            pe.wait_ge(once["cst_loaded"], 16)
            pe.wait_ge(once["first_loaded"], 64)
            for k in range(KD):
                if k >= 2:
                    pe.wait_ge(once["x_turned"], k - 1)
                for t in range(NCH):
                    ins = turn(gslot(k % 2)[:, t * P:(t + 1) * P], xload[:, t, k * P:(k + 1) * P], ident)
                ins.then_inc(once["pe_first"], 1)
            turn(bank(4, 16), prm[0:16, 0, :], ident[0:16, 0:16]).then_inc(once["cond_turned"], 1)
            pe.wait_ge(once["x_turned"], KD)
            pe.wait_ge(once["cond_ready"], 1)

            with pe.Fori(0, L) as l:
                def need(sig, n):
                    pe.wait_ge(sig.sem, sig.at(l, n))

                need(prm_loaded, 16 * PRM_DMAS)
                turn(bank(7, P), prm[:, 0, :], ident)
                turn(ps[:, 3584 + P:3584 + P + NROW2], prm[0:NROW2, 1, :], ident[0:NROW2, 0:NROW2]).then_inc(prm_turned.sem, 1)
                ct = condT.rearrange("p (c k) -> p c k", c=2)
                for i in range(12):
                    need(ring_loaded[i % 3], 16 * (i // 3 + 1))
                    w = ring[i % 3][:, 0:4096].rearrange("p (k n) -> p k n", k=KD)
                    for m in range(4):
                        o = 2048 + (4 * i + m) * 2
                        for k in range(KD):
                            ins = mm(ps[:, o:o + 2], w[:, k, m * P:(m + 1) * P], ct[:, :, k], start=k == 0, stop=k == KD - 1)
                    ins.then_inc(mod_used[i % 3].sem, 1)

                def norm_sums(n):
                    need(mod_ready, 1)
                    for k in range(KD):
                        need(sq_ready, n * KD + k + 1)
                        mm(bank(4), ones, hT[:, k, 0:TS], start=k == 0, stop=k == KD - 1)
                        ins = mm(bank(5, TC), ones, hT[:, k, TS:T], start=k == 0, stop=k == KD - 1)
                    ins.then_inc(norm_ss.sem, 1)

                def gemm(g, lhs, rhs, nk=KD, before=None):
                    need(gemm_out[g % 2], g // 2)
                    o = gslot(g % 2)
                    for k in range(nk):
                        if before:
                            before(k)
                        mm(o[:, 0:TS], lhs(k), rhs(k)[:, 0:TS], start=k == 0, stop=k == nk - 1)
                        ins = mm(o[:, TS:T], lhs(k), rhs(k)[:, TS:T], start=k == 0, stop=k == nk - 1)
                    ins.then_inc(gemm_done.sem, 1)

                norm_sums(0)
                g = 0
                for ci, (o, w) in enumerate(IN_CHUNKS):
                    s = (12 + ci) % 3
                    need(ring_loaded[s], 16 * ((12 + ci) // 3 + 1))
                    wt = ring[s][:, 0:KD * w].rearrange("p (k n) -> p k n", k=KD)
                    if w == 256:
                        for t in range(NCH):
                            for k in range(KD):
                                ins = mm(ps[:, 2048 + 256 * t:2304 + 256 * t], hT[:, k, t * P:(t + 1) * P], wt[:, k, :],
                                         start=k == 0, stop=k == KD - 1)
                        ins.then_inc(v_done.sem, 1)
                        continue
                    for m in range(4):
                        gemm(g, lambda k: wt[:, k, m * P:(m + 1) * P], lambda k: hT[:, k, :],
                             before=(lambda k: need(h_ready, k + 1)) if g == 0 else None)
                        g += 1
                    if ci == 4:
                        need(pT_ready, 1)
                        for t in range(NCH):
                            for k in range(KD):
                                ins = mm(ps[:, 3584 + 16 * t:3600 + 16 * t], hT[:, k, t * P:(t + 1) * P], wab[:, k, :],
                                         start=k == 0, stop=k == KD - 1)
                        ins.then_inc(ab_done.sem, 1)

                need(kvc_loaded, 32)
                need(v_copied, 1)
                for t in range(2):
                    ins = turn(ps[:, 2048 + P * t:2048 + P * (t + 1)], kvc[0][:, P * t:P * (t + 1)], ident)
                ins.then_inc(kc_turned.sem, 1)
                need(gemm_out[1], G_ATT // 2)
                need(gemm_out[0], G_ATT // 2)
                for t in range(2):
                    ins = turn(ps[:, 2560 + P * t:2560 + P * (t + 1)], qkT[:, 2 + t, TS:T], ident)
                ins.then_inc(newk_turned.sem, 1)

                need(conv_out, 1)
                need(ab_copied, 1)
                need(beta_tanh, 1)
                for t in range(2):
                    mm(bank(6), ones, mixA[:, t, 0:TS], start=t == 0, stop=t == 1)
                    ins = mm(bank(7, TC), ones, mixA[:, t, TS + CPAD:CLEN], start=t == 0, stop=t == 1)
                ins.then_inc(ln_sum.sem, 1)
                for t in range(2):
                    need(ln_sq, 2)
                    mm(bank(6), ones, tmp[:, t, 0:TS], start=t == 0, stop=t == 1)
                    ins = mm(bank(7, TC), ones, tmp[:, t, TS + CPAD:CLEN], start=t == 0, stop=t == 1)
                ins.then_inc(ln_var.sem, 1)

                def scores(i):
                    gg = G_ATT + i
                    need(gemm_out[gg % 2], gg // 2)
                    o = gslot(gg % 2)
                    if i < 16:
                        t, h = i // 4, i % 4
                        r = slice(64 * (h % 2), 64 * (h % 2) + 64)
                        qa = qkT[r, h // 2, t * P:(t + 1) * P]
                        mm(o[:, 0:TS], qa, qkT[r, 2 + h // 2, 0:TS], start=True, stop=True)
                        ins = mm(o[:, TS:T], qa, kcT[r, P * (h // 2):P * (h // 2 + 1)], start=True, stop=True)
                    else:
                        for j in range(2):
                            r = slice(64 * j, 64 * j + 64)
                            ins = mm(o[:, TS * j:TS * j + P], qkT[r, i - 16, TS:T], qkT[r, 2 + i - 16, TS:T],
                                     start=True, stop=True)
                    ins.then_inc(gemm_done.sem, 1)

                def turn_probs(i):
                    need(att_n, i + 1)
                    if i >= 1:
                        need(att_ptc, i)
                    for j in range(NCH if i < 16 else 2):
                        ins = turn(ps[:, 2048 + P * j:2048 + P * (j + 1)], sc[i % 2][:, P * j:P * (j + 1)], ident)
                    ins.then_inc(att_pt.sem, 1)

                def values(i):
                    need(att_ptc, i + 1)
                    src = pT_[i % 2]
                    for h in ([i % 4] if i < 16 else [2 * (i - 16), 2 * (i - 16) + 1]):
                        u = i if i < 16 else h + 16
                        r = slice(64 * (h % 2), 64 * (h % 2) + 64)
                        o = ps[r, 512 * (6 + u % 2):512 * (6 + u % 2) + P]
                        if u >= 2:
                            need(att_oc, u - 1)
                        if i < 16:
                            for j in range(NCH):
                                va = vna[:, j, 64 * h:64 * h + 64] if j < 4 else kvc[1][:, 64 * h:64 * h + 64]
                                ins = mm(o, va, src[:, P * j:P * (j + 1)], start=j == 0, stop=j == NCH - 1)
                        else:
                            ins = mm(o, vna[:, 4, 64 * h:64 * h + 64], src[:, P * (h % 2):P * (h % 2 + 1)], start=True, stop=True)
                        ins.then_inc(att_o.sem, 1)

                need(kc_copied, 1)
                need(newk_copied, 1)
                need(ln_r, 1)
                scores(0)
                for i in range(18):
                    if i + 1 < 18:
                        scores(i + 1)
                    turn_probs(i)
                    if i >= 1:
                        values(i - 1)
                values(17)

                def l2_sums(t):
                    need(l2_sq, t + 1)
                    a = 2048 + 1024 * (t % 2)
                    mm(ps[:, a:a + TS], ones, tmp[:, t % 2, 0:TS], start=True, stop=True)
                    mm(ps[:, a + TS:a + T], ones, tmp[:, t % 2, TS + DPAD:DLEN], start=True, stop=True).then_inc(l2_ss.sem, 1)

                def rope(t):
                    need(l2_x, t + 1)
                    if t >= 2:
                        need(rope_x, t - 1)
                    mm(bank(2 * (t % 2)), cst[:, C_PERM:C_PERM + P], dnT[:, t, 0:TS], start=True, stop=True)\
                        .then_inc(rope_mm.sem, 1)

                need(att_ptc, 18)
                need(att_oc, 20)
                need(gemm_out[0], (G_CTX + 2) // 2)
                need(gemm_out[1], (G_CTX + 2) // 2)
                for t in range(9):
                    if t < 8:
                        l2_sums(t)
                    if t >= 1:
                        rope(t - 1)

                for t in range(8):
                    if t < 4:
                        need(rope_x, 4 + t + 1)
                    if t < 2:
                        need(l2_r, 8)
                    else:
                        need(kv_copied, t - 1)
                    for j in range(NCH):
                        a = j * P + (DPAD if j == 4 else 0)
                        ins = turn(ps[:, 2048 + 1024 * (t % 2) + P * j:2048 + 1024 * (t % 2) + P * (j + 1)],
                                   dnT[:, 4 + t, a:a + P], ident)
                    ins.then_inc(kv_turned.sem, 1)
                need(g_ready, 1)
                need(rope_x, 8)
                mm(ps[:, 0:20], cst[:, C_UP:C_UP + P], gsp[:, :, 0:4], start=True, stop=True)
                mm(ps[:, 20:40], cst[:, C_LO:C_LO + P], gsp[:, :, 4:8], start=True, stop=True)
                mm(ps[:, 40:80], ones, gsp[:, :, :], start=True, stop=True).then_inc(gc_done.sem, 1)

                def chunk(j, d):
                    return 4 if j == 4 else (j if d == 0 else 3 - j)

                def cols(cc):
                    a = cc * P + (DPAD if cc == 4 else 0)
                    return slice(a, a + P)

                need(kv_copied, 8)
                need(gc_exp, 1)
                for j in range(5):
                    for d in range(2):
                        u = 2 * j + d
                        cc = chunk(j, d)
                        b0 = 4 * d
                        tri = cst[:, (C_UP, C_LO)[d]:(C_UP, C_LO)[d] + P]
                        if j:
                            need(dn_state, u - 1)
                        for h in range(4):
                            ins = mm(bank(b0)[:, h * P:(h + 1) * P], gsp[:, cc, 4 * d + h:4 * d + h + 1].to_broadcast([P, P]),
                                     tri, start=True, stop=True)
                        ins.then_inc(dn_row.sem, 1)
                        for h in range(4):
                            kk = dnT[:, 4 + h, cols(cc)]
                            mm(bank(b0 + 1)[:, h * P:(h + 1) * P], kk, kk, start=True, stop=True)
                        for h in range(4):
                            kk = dnT[:, 4 + h, cols(cc)]
                            ins = mm(bank(b0 + 2)[:, h * P:(h + 1) * P], kk, dnT[:, h, cols(cc)], start=True, stop=True)
                        ins.then_inc(dn_gram.sem, 1)
                    for d in range(2):
                        u = 2 * j + d
                        need(dn_cs, u // 2 * 2 * LEV + d + 1)
                        need(dn_erow, u + 1)
                        for h in range(4):
                            ins = turn(bank(4 * d)[:, h * P:(h + 1) * P], B[d]["Cs0"][:, h, :], ident)
                        ins.then_inc(dn_c1.sem, 1)
                    for n in range(1, LEV):
                        for d in range(2):
                            need(dn_x, 2 * LEV * j + 2 * (n - 1) + d + 1)
                            need(dn_cs, 2 * LEV * j + 2 * n + d + 1)
                            for h in range(4):
                                ins = mm(bank(4 * d)[:, h * P:(h + 1) * P], B[d][f"Cs{n % 2}"][:, h, :], B[d]["X"][:, h, :],
                                         start=True, stop=True)
                            ins.then_inc(dn_w.sem, 1)
                        for d in range(2):
                            need(dn_wc, 2 * (LEV - 1) * j + 2 * (n - 1) + d + 1)
                            for h in range(4):
                                if n < LEV - 1:
                                    mm(bank(4 * d + 1)[:, h * P:(h + 1) * P], B[d]["XT"][:, h, :], B[d]["W"][:, h, :],
                                       start=True, stop=True)
                            for h in range(4):
                                ins = mm(bank(4 * d + 2)[:, h * P:(h + 1) * P], B[d]["W"][:, h, :], B[d]["XT"][:, h, :],
                                         start=True, stop=True)
                            ins.then_inc(dn_y.sem, 1)
                    for d in range(2):
                        cc = chunk(j, d)
                        if j == 0:
                            need(state_loaded, 32)
                        else:
                            need(dn_state, 2 * j)
                        if j == 4:
                            need(ctx_zero, d + 1)
                        need(dn_x, 2 * LEV * (j + 1) - 1 + d)
                        for h in range(4):
                            ins = mm(bank(4 * d + 1)[:, h * P:(h + 1) * P], dnT[:, 4 + h, cols(cc)], S[d][:, h, :],
                                     start=True, stop=True)
                        ins.then_inc(dn_ks.sem, 1)
                    for d in range(2):
                        need(dn_res, 2 * j + d + 1)
                        for h in range(4):
                            ins = mm(bank(4 * d + 2)[:, h * P:(h + 1) * P], B[d]["XT"][:, h, :], B[d]["CT"][:, h, :],
                                     start=True, stop=True)
                        ins.then_inc(dn_u.sem, 1)
                    for d in range(2):
                        need(dn_uu, 2 * j + d + 1)
                        need(dn_qk, 4 * j + 2 * d + 2)
                        for h in range(4):
                            o = bank(4 * d + 3)[:, h * P:(h + 1) * P]
                            mm(o, S[d][:, h, :], B[d]["qdec"][:, h, :], start=True, stop=False)
                            mm(o, B[d]["W"][:, h, :], B[d]["aqk"][:, h, :], start=False, stop=True)
                        for h in range(4):
                            ins = mm(bank(4 * d + 1)[:, h * P:(h + 1) * P], B[d]["kdec"][:, h, :], B[d]["W"][:, h, :],
                                     start=True, stop=True)
                        ins.then_inc(dn_o.sem, 1)

                need(dn_state, 10)
                for h in range(4):
                    need(on_sq, h + 1)
                    if h >= 2:
                        need(on_r, h - 1)
                    a = 2048 + 1024 * (h % 2)
                    mm(ps[:, a:a + TS], ones, tmp[:, h % 2, 0:TS], start=True, stop=True)
                    mm(ps[:, a + TS:a + T], ones, tmp[:, h % 2, TS + DPAD:DLEN], start=True, stop=True).then_inc(on_ss.sem, 1)

                need(mixa_ready, 2)

                def mix(k):
                    if k < 2:
                        return (mixA[:, k, 0:TS], mixA[:, k, TS + CPAD:CLEN])
                    if k < 4:
                        return (mixB[:, k - 2, 0:TS], mixB[:, k - 2, TS:T])
                    return (dnT[:, 4 + k, 0:TS], dnT[:, 4 + k, TS + DPAD:DLEN])

                for m in range(KD):
                    gg = G_OUT + m
                    s = (19 + m // 4) % 3
                    if m % 4 == 0:
                        need(ring_loaded[s], 16 * ((19 + m // 4) // 3 + 1))
                    wt = ring[s][:, 0:4096].rearrange("p (k n) -> p k n", k=KD)
                    need(gemm_out[gg % 2], gg // 2)
                    for k in range(KD):
                        if m == 0 and k >= 4:
                            need(mixc_ready, k - 3)
                        lhs = wt[:, k, (m % 4) * P:(m % 4 + 1) * P]
                        mm(gslot(gg % 2)[:, 0:TS], lhs, mix(k)[0], start=k == 0, stop=k == KD - 1)
                        ins = mm(gslot(gg % 2)[:, TS:T], lhs, mix(k)[1], start=k == 0, stop=k == KD - 1)
                    ins.then_inc(gemm_done.sem, 1)

                norm_sums(1)
                for t in range(NCH):
                    for k in range(KD):
                        if t == 0:
                            need(h_ready, KD + k + 1)
                        ins = mm(ps[:, 3072 + 20 * t:3092 + 20 * t], hT[:, k, t * P:(t + 1) * P], wr[:, k, :],
                                 start=k == 0, stop=k == KD - 1)
                ins.then_inc(logits.sem, 1)
                need(gates_ready, 1)
                gv = rt[:, 0:80].rearrange("p (c e) -> p c e", c=NCH)
                for t in range(NCH):
                    ins = turn(ps[0:NE, 2048 + P * t:2048 + P * (t + 1)], gv[:, t, :], ident)
                ins.then_inc(gates_turned.sem, 1)

                def experts(pr):
                    def need_pair(sig, n, per):
                        pe.wait_ge(sig.sem, sig.at(l, n) + pr * per)

                    for q in range(2):
                        need_pair(ring_loaded[q], 16 * 7 + 32, 32)
                        for f in range(FT):
                            for m in range(2):
                                gg = G_MOE + 12 * q + 2 * f + m
                                need_pair(gemm_out[m], gg // 2, G_PAIR // 2)
                                wt = ring[q][:, 2048 * m:2048 * m + 2048].rearrange("p (k n) -> p k n", k=KD)
                                for k in range(KD):
                                    lhs = wt[:, k, f * P:(f + 1) * P]
                                    mm(gslot(m)[:, 0:TS], lhs, hT[:, k, 0:TS], start=k == 0, stop=k == KD - 1)
                                    ins = mm(gslot(m)[:, TS:T], lhs, hT[:, k, TS:T], start=k == 0, stop=k == KD - 1)
                                ins.then_inc(gemm_done.sem, 1)
                        need_pair(w2_loaded[q], 16, 16)
                        need_pair(hid_ready, 2 * q + 2, 4)
                        wt = ring[2][:, 2048 * q:2048 * q + 2048].rearrange("p (k n) -> p k n", k=FT)
                        for m in range(KD):
                            gg = G_MOE + 12 * q + 4 + m
                            need_pair(gemm_out[m % 2], gg // 2, G_PAIR // 2)
                            for k in range(FT):
                                lhs = wt[:, k, m * P:(m + 1) * P]
                                mm(gslot(m % 2)[:, 0:TS], lhs, hid[2 * q + k][:, 0:TS], start=k == 0, stop=k == FT - 1)
                                ins = mm(gslot(m % 2)[:, TS:T], lhs, hid[2 * q + k][:, TS:T], start=k == 0, stop=k == FT - 1)
                            ins.then_inc(gemm_done.sem, 1)

                with pe.Fori(0, NE // 2) as pr:
                    experts(pr)

            for k in range(KD):
                pe.wait_ge(once["fin_sq"], k + 1)
                mm(bank(4), ones, hT[:, k, 0:TS], start=k == 0, stop=k == KD - 1)
                ins = mm(bank(5, TC), ones, hT[:, k, TS:T], start=k == 0, stop=k == KD - 1)
            ins.then_inc(once["fin_ss"], 1)
            for k in range(KD):
                pe.wait_ge(once["fin_y"], k + 1)
                if k >= 2:
                    pe.wait_ge(once["y_copied"], k - 1)
                for t in range(NCH):
                    ins = turn(gslot(k % 2)[:, t * P:(t + 1) * P], xT[:, k, t * P:(t + 1) * P], ident)
                ins.then_inc(once["y_turned"], 1)

        @block.scalar
        def _(act):
            A_ = nc.scalar.activation
            act.wait_ge(once["cst_loaded"], 16)
            act.wait_ge(once["cond_turned"], 1)
            A_(condT, bank(4, 16), ACT.Silu).then_inc(once["cond_ready"], 1)
            act.wait_ge(once["cond_ready"], 1)
            act.wait_ge(once["x_turned"], KD)
            act.wait_ge(once["pads_written"], 32)

            with act.Fori(0, L) as l:
                n_step = [0]

                def need(sig, n):
                    act.wait_ge(sig.sem, sig.at(l, n))

                def step(ins):
                    n_step[0] += 1
                    ins.then_inc(act_step.sem, 1)
                    need(act_step, n_step[0])

                need(gemm_out[0], 0)
                need(gemm_out[1], 0)
                loads = [
                    (prm[R_BMOD:R_BMOD + 48, 0, :], b_mod[l].rearrange("(r p) -> r p", p=P)),
                    (prm[R_G1:R_G1 + 8, 0, :], g1[l].rearrange("(r p) -> r p", p=P)),
                    (prm[R_G2:R_G2 + 8, 0, :], g2[l].rearrange("(r p) -> r p", p=P)),
                    (prm[R_CW:R_CW + 62, 0, :], conv_w[l].rearrange("k (r p) -> (k r) p", p=P)),
                    (prm[R_CB:R_CB + 2, 0, :], conv_b[l].rearrange("(r p) -> r p", p=P)),
                    (prm[0:2, 1, :], ln_g[l].rearrange("(r p) -> r p", p=P)),
                    (prm[2:4, 1, :], ln_b[l].rearrange("(r p) -> r p", p=P)),
                    (prm[4:64, 1, :], dn_conv_w[l].rearrange("k (r p) -> (k r) p", p=P)),
                    (prm[64:65, 1, :], norm_g[bass.ds(l, 1), :]),
                    (prm[65:73, 1, :], g_final.rearrange("(r p) -> r p", p=P)),
                    (alog, a_log[l].rearrange("(a n) -> a n", a=1).to_broadcast([P, 8])),
                    (dtb, dt_bias[l].rearrange("(a n) -> a n", a=1).to_broadcast([P, 8])),
                    (rbias[:, 0:4], bg[bass.ds(l, 1), :].to_broadcast([P, 4])),
                    (rbias[:, 4:20], be[bass.ds(l, 1), :].to_broadcast([P, 16])),
                    (wr[:, :, 0:4], wg[l].rearrange("(k p) n -> p k n", p=P)),
                    (wab, w_in[l][:, OFF_AB:PROJ].rearrange("(k p) n -> p k n", p=P)),
                    (wr[:, :, 4:20], we[l].rearrange("(k p) n -> p k n", p=P)),
                ]
                assert len(loads) == PRM_DMAS
                for dst, src in loads:
                    act.dma_start(dst, src).then_inc(prm_loaded.sem, 16)
                act.dma_start(bias_pad.ap()[:, GRID:GRID + NB],
                              rel_bias[l].rearrange("(a n) -> a n", a=1).to_broadcast([GRID, NB])).then_inc(bias_copied.sem, 16)

                def norm(n):
                    for k in range(KD):
                        A_(hT[:, k, :], xT[:, k, :], ACT.Square).then_inc(sq_ready.sem, 1)
                    need(norm_ss, n + 1)
                    step(A_(rst[:, 0:T], ps[:, 2048:2048 + T], ACT.Ln, scale=1.0 / D, bias=eps_c))
                    A_(rst[:, 0:T], rst[:, 0:T], ACT.Exp, scale=-0.5).then_inc(norm_r.sem, 1)
                    sh = 24 * n
                    for k in range(KD):
                        need(norm_x, n * KD + k + 1)
                        A_(hT[:, k, 0:TS], hT[:, k, 0:TS], ACT.Identity, scale=A[n][:, k, 0:1], bias=mod[:, sh + k, 0:1])
                        A_(hT[:, k, TS:T], hT[:, k, TS:T], ACT.Identity, scale=A[n][:, k, 1:2], bias=mod[:, sh + k, 1:2])\
                            .then_inc(h_ready.sem, 1)

                nc.scalar.preload_act_table_set("natural_log_exp_and_others")
                norm(0)
                need(bias_copied, 16)
                lo = bass.AP(tensor=bias_pad, offset=GRID + 15, ap=[[BP - 1, GRID], [CO, NH * RO], [1, GRID]])
                act.dma_start(tzv[0:GRID], lo).then_inc(bias_loaded.sem, 16)
                hi = bass.AP(tensor=bias_pad, offset=GRID + 15, ap=[[BP - 1, GRID], [CO, NH * RO - 1], [1, GRID]])
                act.dma_start(tzv[GRID:P, 1:NH * RO, :], hi).then_inc(bias_loaded.sem, 16)

                def evac(g, out, func=ACT.Copy, scale=1.0):
                    need(gemm_done, g + 1)
                    return A_(out, gslot(g % 2), func, scale=scale)

                for t in range(2):
                    evac(G_GLU + t, dnT[:, 10 + t, 0:T], scale=0.5).then_inc(gemm_out[t].sem, 1)
                for t in range(2):
                    evac(G_GLU + 2 + t, zs[:, t, :], ACT.Tanh, 0.5).then_inc(gemm_out[t].sem, 1)

                def dn_silu_of(t):
                    need(dn_conv, t + 1)
                    if t == 10:
                        need(conv_in, 2)
                    A_(dnT[:, t, 0:DLEN], tmp[:, t % 2, 0:DLEN], ACT.Silu).then_inc(dn_silu.sem, 1)

                need(pads_zeroed, 1)
                for t in range(12):
                    g = G_DN + t
                    need(gemm_done, g + 1)
                    if t >= 2:
                        need(dn_conv, t - 1)
                    A_(stage[t % 2][:, DPAD:DPAD + TS], gslot(g % 2)[:, 0:TS], ACT.Copy)
                    A_(stage[t % 2][:, 2 * DPAD + TS:2 * DPAD + T], gslot(g % 2)[:, TS:T], ACT.Copy)\
                        .then_inc(gemm_out[g % 2].sem, 1)
                    if t >= 1:
                        dn_silu_of(t - 1)
                need(conv_in, 2)
                for t in range(4):
                    evac(G_Z + t, zs[:, t, :], ACT.Silu).then_inc(gemm_out[t % 2].sem, 1)
                    if t == 0:
                        dn_silu_of(11)
                need(ab_done, 1)
                A_(ab, ps[:, 3584:3664].rearrange("p (c n) -> p c n", c=NCH), ACT.Copy).then_inc(ab_copied.sem, 1)
                need(ab_copied, 1)
                A_(beta, ab[:, :, 8:16], ACT.Tanh, scale=0.5)\
                    .then_inc(beta_tanh.sem, 1)
                for t in range(4):
                    evac(G_QK + t, qkT[:, t, :]).then_inc(gemm_out[t % 2].sem, 1)
                need(v_done, 1)
                A_(vna.rearrange("p t n -> p (t n)"), ps[:, 2048:2048 + NCH * NAW], ACT.Copy).then_inc(v_copied.sem, 1)
                for i, cache in enumerate((cache_k, cache_v)):
                    act.dma_start(kvc[i], cache[l].rearrange("s h d -> s (h d)")).then_inc(kvc_loaded.sem, 16)
                need(kc_turned, 1)
                A_(kcT, ps[:, 2048:2048 + 256], ACT.Copy).then_inc(kc_copied.sem, 1)
                need(newk_turned, 1)
                A_(newk, ps[:, 2560:2560 + 256], ACT.Copy).then_inc(newk_copied.sem, 1)
                need(newk_copied, 1)
                act.dma_start(new_k[l].rearrange("s h d -> s (h d)"), newk).then_inc(newkv_stored.sem, 16)
                need(v_copied, 1)
                act.dma_start(new_v[l].rearrange("s h d -> s (h d)"), vna[:, 4, :]).then_inc(newkv_stored.sem, 16)

                nc.scalar.preload_act_table_set("natural_log_exp_and_others")
                need(g_abs, 1)
                step(A_(gt1, gsp, ACT.Abs))
                step(A_(gt1, gt1, ACT.Exp, scale=-1.0))
                A_(gt1, gt1, ACT.Ln, bias=one_c)
                A_(ealog, alog, ACT.Exp).then_inc(g_act.sem, 1)
                need(conv_out, 1)
                for d in range(2):
                    act.dma_start(S[d], state[l, d].rearrange("h k v -> k h v")).then_inc(state_loaded.sem, 16)

                for t in range(2):
                    need(ln_xc, t + 1)
                    A_(tmp[:, t, :], mixA[:, t, :], ACT.Square).then_inc(ln_sq.sem, 1)
                need(ln_var, 1)
                step(A_(rst[:, 0:T], ps[:, 3072:3072 + T], ACT.Ln, scale=1.0 / CW, bias=eps_c))
                A_(rst[:, 0:T], rst[:, 0:T], ACT.Exp, scale=-0.5).then_inc(ln_r.sem, 1)
                for t in range(2):
                    need(ln_y, t + 1)
                    A_(mixA[:, t, :], mixA[:, t, :], ACT.Silu).then_inc(mixa_ready.sem, 1)
                nc.scalar.preload_act_table_set("natural_log_exp_and_others")

                def att_probs(i):
                    need(att_s, i + 1)
                    if i < 16:
                        A_(sc[i % 2], sc[i % 2], ACT.Exp, bias=st[:, i % 2:i % 2 + 1],
                           accum_out=st[:, 4 + i % 2:5 + i % 2]).then_inc(att_p.sem, 1)
                    else:
                        for j in range(2):
                            ins = A_(sc[i % 2][:, P * j:P * (j + 1)], sc[i % 2][:, P * j:P * (j + 1)], ACT.Exp,
                                     bias=st[:, 8 + 2 * (i % 2) + j:9 + 2 * (i % 2) + j],
                                     accum_out=st[:, 12 + 2 * (i % 2) + j:13 + 2 * (i % 2) + j])
                        ins.then_inc(att_p.sem, 1)

                def att_copy(i):
                    need(att_pt, i + 1)
                    if i >= 2:
                        need(att_o, i - 1)
                    n = T if i < 16 else 2 * P
                    A_(pT_[i % 2][:, 0:n], ps[:, 2048:2048 + n], ACT.Copy).then_inc(att_ptc.sem, 1)

                def att_store(i):
                    for h in ([i % 4] if i < 16 else [2 * (i - 16), 2 * (i - 16) + 1]):
                        u = i if i < 16 else h + 16
                        need(att_o, u + 1)
                        r = slice(64 * (h % 2), 64 * (h % 2) + 64)
                        t = slice((i // 4) * P, (i // 4 + 1) * P) if i < 16 else slice(TS, T)
                        A_(mixB[r, h // 2, t], ps[r, 512 * (6 + u % 2):512 * (6 + u % 2) + P], ACT.Copy).then_inc(att_oc.sem, 1)

                for i in range(18):
                    att_probs(i)
                    att_copy(i)
                    if i >= 1:
                        att_store(i - 1)
                att_store(17)

                for t in range(9):
                    if t < 8:
                        if t >= 2:
                            need(l2_ss, t - 1)
                        A_(tmp[:, t % 2, 0:DLEN], dnT[:, t, 0:DLEN], ACT.Square).then_inc(l2_sq.sem, 1)
                    if t >= 1:
                        u = t - 1
                        need(l2_ss, u + 1)
                        a = 2048 + 1024 * (u % 2)
                        if u >= 1:
                            need(l2_x, u)
                        step(A_(rst[:, 0:T], ps[:, a:a + T], ACT.Ln, bias=eps_c))
                        if u < 4:
                            A_(rst[:, 0:T], rst[:, 0:T], ACT.Exp, scale=-0.5, bias=lnsc_c).then_inc(l2_r.sem, 1)
                        else:
                            A_(rst[:, 0:T], rst[:, 0:T], ACT.Exp, scale=-0.5).then_inc(l2_r.sem, 1)
                need(att_s, 18)
                for t in range(8):
                    need(kv_turned, t + 1)
                    A_(tok[:, t // 4, :, P * (t % 4):P * (t % 4 + 1)],
                       ps[:, 2048 + 1024 * (t % 2):2048 + 1024 * (t % 2) + T].rearrange("p (c n) -> p c n", c=NCH),
                       ACT.Copy).then_inc(kv_copied.sem, 1)
                need(gc_copied, 1)
                A_(egc, gcum[:, 0:40], ACT.Exp)
                A_(ekd, ekd, ACT.Exp)
                A_(cdec, gcum[:, 40:80], ACT.Exp).then_inc(gc_exp.sem, 1)

                for j in range(5):
                    for d in range(2):
                        u = 2 * j + d
                        need(dn_row, u + 1)
                        if j == 0:
                            need(newkv_stored, 32)
                        if j:
                            need(dn_o, u - 1)
                        need(dn_dlog, u + 1)
                        A_(B[d]["DT"], B[d]["DT"], ACT.Exp).then_inc(dn_dexp.sem, 1)
                        A_(B[d]["qdec"], heads(bank(4 * d)), ACT.Exp).then_inc(dn_erow.sem, 1)
                    for n in range(1, LEV):
                        for d in range(2):
                            need(dn_w, 2 * (LEV - 1) * j + 2 * (n - 1) + d + 1)
                            A_(B[d]["W"], heads(bank(4 * d)), ACT.Copy).then_inc(dn_wc.sem, 1)
                for d in range(2):
                    need(dn_state, 9 + d)
                    act.dma_start(new_s[l, d].rearrange("h k v -> k h v"), S[d]).then_inc(state_stored.sem, 16)

                for h in range(5):
                    if h < 4:
                        if h >= 2:
                            need(on_ss, h - 1)
                        A_(tmp[:, h % 2, 0:DLEN], dnT[:, 8 + h, 0:DLEN], ACT.Square).then_inc(on_sq.sem, 1)
                    if h >= 1:
                        u = h - 1
                        need(on_ss, u + 1)
                        if u >= 1:
                            need(mixc_ready, u)
                        a = 2048 + 1024 * (u % 2)
                        step(A_(rst[:, 0:T], ps[:, a:a + T], ACT.Ln, scale=1.0 / DK, bias=eps_c))
                        A_(rst[:, 0:T], rst[:, 0:T], ACT.Exp, scale=-0.5).then_inc(on_r.sem, 1)

                need(state_stored, 32)
                need(gemm_out[0], (G_OUT + 8) // 2)
                need(gemm_out[1], (G_OUT + 8) // 2)
                norm(1)
                need(rt_in, 1)
                A_(rt[:, 180:200], rt[:, 180:200], ACT.Exp).then_inc(rt_exp.sem, 1)
                need(rt_in2, 1)
                A_(rt[:, 350:355], rt[:, 350:355], ACT.Exp).then_inc(rt_exp2.sem, 1)
                need(gates_turned, 1)
                A_(gT, ps[0:NE, 2048:2048 + T], ACT.Copy).then_inc(gates_copied.sem, 1)
                need(gates_copied, 1)
                act.dma_start(gate_rows, gT).then_inc(gates_stored.sem, 16)

                with act.Fori(0, NE // 2) as pr:
                    for q in range(2):
                        for f in range(FT):
                            g = G_MOE + 12 * q + 2 * f
                            act.wait_ge(gemm_done.sem, gemm_done.at(l, g + 1) + pr * G_PAIR)
                            act.wait_ge(hid_ready.sem, hid_ready.at(l, 2 * q + f - 1) + pr * 4)
                            A_(sil[f], gslot(0), ACT.Silu).then_inc(gemm_out[0].sem, 1)

            assert n_step[0] == ACT_STEPS, n_step
            act.wait_ge(gemm_out[0].sem, gemm_out[0].at(L, 0))
            act.wait_ge(gemm_out[1].sem, gemm_out[1].at(L, 0))
            nc.scalar.preload_act_table_set("natural_log_exp_and_others")
            for k in range(KD):
                A_(hT[:, k, :], xT[:, k, :], ACT.Square).then_inc(once["fin_sq"], 1)
            act.wait_ge(once["fin_ss"], 1)
            A_(rst[:, 0:T], ps[:, 2048:2048 + T], ACT.Ln, scale=1.0 / D, bias=eps_c).then_inc(once["fin_r"], 1)
            act.wait_ge(once["fin_r"], 1)
            A_(rst[:, 0:T], rst[:, 0:T], ACT.Exp, scale=-0.5).then_inc(once["fin_r"], 1)
            yt = xload
            for k in range(KD):
                act.wait_ge(once["y_turned"], k + 1)
                A_(yt[:, :, k * P:(k + 1) * P], gslot(k % 2).rearrange("p (c n) -> p c n", c=NCH), ACT.Copy)\
                    .then_inc(once["y_copied"], 1)
            act.wait_ge(once["y_copied"], KD)
            act.dma_start(y_sample[0].rearrange("(c p) d -> p c d", p=P), yt[:, 0:4, :]).then_inc(once["y_stored"], 16)
            act.dma_start(y_prompt[0], yt[:, 4, :]).then_inc(once["y_stored"], 16)
            act.wait_ge(newkv_stored.sem, 32 * L)
            act.wait_ge(state_stored.sem, 32 * L)
            act.wait_ge(once["y_stored"], 32)

        @block.vector
        def _(dve):
            V = nc.vector
            V.memset(rst[:, 0:GRID], 0.0).then_inc(once["pad_ready"], 1)
            for k in range(KD):
                dve.wait_ge(once["pe_first"], k + 1)
                V.tensor_copy(xT[:, k, :], gslot(k % 2)).then_inc(once["x_turned"], 1)
            for s in gemm_out:
                dve.sem_inc(s.sem, 1)
            dve.sem_inc(hid_ready.sem, 2)
            dve.wait_ge(once["x_turned"], KD)
            dve.wait_ge(once["pads_written"], 32)

            with dve.Fori(0, L) as l:
                n_step = [0]

                def need(sig, n):
                    dve.wait_ge(sig.sem, sig.at(l, n))

                def count(ins):
                    n_step[0] += 1
                    ins.then_inc(dve_step.sem, 1)
                    return n_step[0]

                def step(ins):
                    need(dve_step, count(ins))

                need(gemm_done, 0)
                for s in stage:
                    V.memset(s, 0.0)
                V.memset(cin_reg[:, :], 0.0).then_inc(pads_zeroed.sem, 1)
                need(prm_turned, 1)
                V.tensor_copy(pT, ps[:, 3584:3584 + 201]).then_inc(pT_ready.sem, 1)
                need(pT_ready, 1)
                need(mod_used[2], 4)
                both = pT.rearrange("p (r a) -> p r a", a=1)
                step(V.tensor_tensor(mod, ps[:, 2048:2144].rearrange("p (j c) -> p j c", c=2),
                                     both[:, 0:48].to_broadcast([P, 48, 2]), ALU.add))
                V.scalar_tensor_tensor(A[0], mod[:, 8:16, :], 1.0, both[:, R_G1:R_G1 + KD].to_broadcast([P, KD, 2]),
                                       ALU.add, ALU.mult)
                V.scalar_tensor_tensor(A[1], mod[:, 32:40, :], 1.0, both[:, R_G2:R_G2 + KD].to_broadcast([P, KD, 2]),
                                       ALU.add, ALU.mult).then_inc(mod_ready.sem, 1)

                def norm(n):
                    need(norm_r, n + 1)
                    for k in range(KD):
                        V.tensor_tensor(hT[:, k, :], xT[:, k, :], rst, ALU.mult).then_inc(norm_x.sem, 1)

                norm(0)
                need(pads_zeroed, 1)
                for t in range(2):
                    need(gemm_out[t], 2)
                    V.scalar_tensor_tensor(cin[:, t, CPAD:CPAD + TS], zs[:, t, 0:TS], 1.0, dnT[:, 10 + t, 0:TS],
                                           ALU.add, ALU.mult)
                    V.scalar_tensor_tensor(cin[:, t, 2 * CPAD + TS:2 * CPAD + T], zs[:, t, TS:T], 1.0,
                                           dnT[:, 10 + t, TS:T], ALU.add, ALU.mult).then_inc(conv_in.sem, 1)
                need(conv_in, 2)

                taps = [(k, t) for k in range(CK) for t in range(2)]
                last = [0, 0]

                def conv_tap():
                    if not taps:
                        return
                    k, t = taps.pop(0)
                    w = pT[:, R_CW + 2 * k + t:R_CW + 2 * k + t + 1]
                    src = cin[:, t, k:k + CLEN]
                    if k == 0:
                        last[t] = count(V.tensor_scalar(mixA[:, t, :], src, w, None, ALU.mult))
                    else:
                        need(dve_step, last[t])
                        last[t] = count(V.scalar_tensor_tensor(mixA[:, t, :], src, w, mixA[:, t, :], ALU.mult, ALU.add))

                for t in range(12):
                    need(gemm_out[t % 2], (G_DN + t) // 2 + 1)
                    if t >= 2:
                        need(dn_silu, t - 1)
                    out = tmp[:, t % 2, 0:DLEN]
                    for k in range(DCK):
                        w = pT[:, R_DW + 12 * k + t:R_DW + 12 * k + t + 1]
                        src = stage[t % 2][:, k:k + DLEN]
                        if k == 0:
                            n = count(V.tensor_scalar(out, src, w, None, ALU.mult))
                        else:
                            need(dve_step, n)
                            ins = V.scalar_tensor_tensor(out, src, w, out, ALU.mult, ALU.add)
                            if k == DCK - 1:
                                ins.then_inc(dn_conv.sem, 1)
                            else:
                                n = count(ins)
                        conv_tap()
                while taps:
                    conv_tap()
                need(dve_step, n_step[0])
                for t in range(2):
                    ins = V.tensor_scalar(mixA[:, t, :], mixA[:, t, :], pT[:, R_CB + t:R_CB + t + 1], None, ALU.add)
                ins.then_inc(conv_out.sem, 1)

                need(ab_copied, 1)
                row = dtb.rearrange("p (a n) -> p a n", a=1).to_broadcast([P, NCH, 8])
                V.tensor_tensor(gsp, ab[:, :, 0:8], row, ALU.add).then_inc(g_abs.sem, 1)
                need(g_act, 1)
                step(V.scalar_tensor_tensor(gsp, gsp, 0.0, gt1, ALU.max, ALU.add))
                row = ealog.rearrange("p (a n) -> p a n", a=1).to_broadcast([P, NCH, 8])
                V.scalar_tensor_tensor(gsp, gsp, -1.0, row, ALU.mult, ALU.mult)
                need(beta_tanh, 1)
                V.tensor_scalar(beta, beta, 0.5, 0.5, ALU.mult, ALU.add).then_inc(g_ready.sem, 1)

                need(conv_out, 1)
                need(ln_sum, 1)
                parts = ((slice(0, TS), slice(0, TS)), (slice(TS + CPAD, CLEN), slice(TS, T)))
                for t in range(2):
                    for a, b in parts:
                        ins = V.scalar_tensor_tensor(mixA[:, t, a], ps[:, 3072:3072 + T][:, b], -1.0 / CW, mixA[:, t, a],
                                                     ALU.mult, ALU.add)
                    ins.then_inc(ln_xc.sem, 1)
                need(ln_r, 1)
                for t in range(2):
                    for a, b in parts:
                        ins = V.scalar_tensor_tensor(mixA[:, t, a], mixA[:, t, a], pT[:, R_LNG + t:R_LNG + t + 1], rst[:, b],
                                                     ALU.mult, ALU.mult)
                    step(ins)
                    V.tensor_scalar(mixA[:, t, :], mixA[:, t, :], pT[:, R_LNB + t:R_LNB + t + 1], None, ALU.add)\
                        .then_inc(ln_y.sem, 1)

                need(tz_ready, 1)

                def att_scores(i):
                    gg = G_ATT + i
                    need(gemm_done, gg + 1)
                    if i >= 2:
                        need(att_pt, i - 1)
                    o, s = gslot(gg % 2), sc[i % 2]
                    if i < 16:
                        t, h = i // 4, i % 4
                        b = h * RO + 7 - 2 * t
                        V.scalar_tensor_tensor(s[:, 0:TS], o[:, 0:TS], HD ** -0.5, Tz[:, b * GRID:b * GRID + TS], ALU.mult, ALU.add)
                        V.tensor_scalar(s[:, TS:T], o[:, TS:T], HD ** -0.5, None, ALU.mult).then_inc(gemm_out[gg % 2].sem, 1)
                        need(gemm_out[gg % 2], gg // 2 + 1)
                        step(V.tensor_reduce(st[:, i % 2:i % 2 + 1], s, AX, ALU.max))
                        m = st[:, i % 2:i % 2 + 1]
                    else:
                        V.tensor_scalar(s[:, 0:P], o[:, 0:P], HD ** -0.5, None, ALU.mult)
                        V.tensor_scalar(s[:, P:2 * P], o[:, TS:T], HD ** -0.5, None, ALU.mult).then_inc(gemm_out[gg % 2].sem, 1)
                        need(gemm_out[gg % 2], gg // 2 + 1)
                        m = st[:, 8 + 2 * (i % 2):10 + 2 * (i % 2)]
                        step(V.tensor_reduce(m, s[:, 0:2 * P].rearrange("p (h n) -> p h n", h=2), AX, ALU.max))
                    V.tensor_scalar(m, m, -1.0, None, ALU.mult).then_inc(att_s.sem, 1)

                def att_norm(i):
                    need(att_p, i + 1)
                    s = sc[i % 2]
                    if i < 16:
                        r = st[:, 6 + i % 2:7 + i % 2]
                        step(V.reciprocal(r, st[:, 4 + i % 2:5 + i % 2]))
                        V.tensor_scalar(s, s, r, None, ALU.mult).then_inc(att_n.sem, 1)
                    else:
                        r = st[:, 12 + 2 * (i % 2):14 + 2 * (i % 2)]
                        step(V.reciprocal(r, r))
                        for j in range(2):
                            ins = V.tensor_scalar(s[:, P * j:P * (j + 1)], s[:, P * j:P * (j + 1)], r[:, j:j + 1], None, ALU.mult)
                        ins.then_inc(att_n.sem, 1)

                att_scores(0)
                for i in range(18):
                    if i + 1 < 18:
                        att_scores(i + 1)
                    att_norm(i)

                for t in range(9):
                    if t < 8:
                        need(l2_r, t + 1)
                        V.tensor_tensor(dnT[:, t, 0:TS], dnT[:, t, 0:TS], rst[:, 0:TS], ALU.mult)
                        V.tensor_tensor(dnT[:, t, TS + DPAD:DLEN], dnT[:, t, TS + DPAD:DLEN], rst[:, TS:T], ALU.mult)\
                            .then_inc(l2_x.sem, 1)
                    if t >= 1:
                        u = t - 1
                        need(rope_mm, u + 1)
                        need(rope_cos, u + 1)
                        if u:
                            need(rope_x, u)
                        step(V.tensor_tensor(rsin, bank(2 * (u % 2)), cst[:, C_SIN:C_SIN + TS], ALU.mult))
                        V.tensor_tensor(dnT[:, u, 0:TS], rcos[u % 2], rsin, ALU.add).then_inc(rope_x.sem, 1)
                need(gc_done, 1)
                step(V.tensor_copy(gcum, ps[:, 0:80]))
                tot = gcum[:, 40:80].rearrange("p (c d h) -> p d c h", c=NCH, d=2)
                V.tensor_tensor(ekd.rearrange("p (d c h) -> p d c h", d=2, c=NCH), tot,
                                gcum[:, 0:40].rearrange("p (d c h) -> p d c h", d=2, c=NCH), ALU.subtract)\
                    .then_inc(gc_copied.sem, 1)
                need(gc_exp, 1)
                step(V.tensor_scalar(egc, egc, -1.0, None, ALU.mult))

                def chunk(j, d):
                    return 4 if j == 4 else (j if d == 0 else 3 - j)

                def col(ap, d, cc, h):
                    i = 20 * d + 4 * cc + h
                    return ap[:, i:i + 1]

                need(newkv_stored, 32)
                for j in range(5):
                    for d in range(2):
                        need(dn_row, 2 * j + d + 1)
                        for h in range(4):
                            ins = V.tensor_scalar(B[d]["DT"][:, h, :], bank(4 * d)[:, h * P:(h + 1) * P],
                                                  col(gcum, d, chunk(j, d), h), 0.0, ALU.subtract, ALU.min)
                        ins.then_inc(dn_dlog.sem, 1)
                    for d in range(2):
                        cc = chunk(j, d)
                        need(dn_dexp, 2 * j + d + 1)
                        need(dn_gram, 2 * j + d + 1)
                        tri = cst[:, (C_UP, C_LO)[d]:(C_UP, C_LO)[d] + P]
                        step(V.tensor_tensor(B[d]["DT"], B[d]["DT"], over_heads(tri), ALU.mult))
                        for h in range(4):
                            V.scalar_tensor_tensor(B[d]["CT"][:, h, :], bank(4 * d + 1)[:, h * P:(h + 1) * P],
                                                   beta[:, cc, 4 * d + h:4 * d + h + 1], B[d]["DT"][:, h, :], ALU.mult, ALU.mult)
                        V.tensor_tensor(B[d]["aqk"], heads(bank(4 * d + 2)), B[d]["DT"], ALU.mult).then_inc(dn_mat.sem, 1)
                    for d in range(2):
                        need(dn_c1, 2 * j + d + 1)
                        V.tensor_tensor(B[d]["X"], over_heads(ident), heads(bank(4 * d)), ALU.subtract)
                        V.tensor_tensor(B[d]["XT"], over_heads(ident), B[d]["Cs0"], ALU.subtract).then_inc(dn_x.sem, 1)
                    for n in range(1, LEV):
                        for d in range(2):
                            need(dn_y, 2 * (LEV - 1) * j + 2 * (n - 1) + d + 1)
                            if n < LEV - 1:
                                V.tensor_tensor(B[d]["X"], B[d]["X"], heads(bank(4 * d + 1)), ALU.subtract)
                            V.tensor_tensor(B[d]["XT"], B[d]["XT"], heads(bank(4 * d + 2)), ALU.subtract).then_inc(dn_x.sem, 1)
                    for d in range(2):
                        cc = chunk(j, d)
                        need(dn_ks, 2 * j + d + 1)
                        for h in range(4):
                            ins = V.scalar_tensor_tensor(B[d]["CT"][:, h, :], bank(4 * d + 1)[:, h * P:(h + 1) * P],
                                                         col(egc, d, cc, h), tok[:, 1, cc, h * P:(h + 1) * P], ALU.mult, ALU.add)
                        ins.then_inc(dn_res.sem, 1)
                    for d in range(2):
                        cc = chunk(j, d)
                        need(dn_u, 2 * j + d + 1)
                        V.tensor_tensor(B[d]["W"], heads(bank(4 * d + 2)), along(beta[:, cc, 4 * d:4 * d + 4], P), ALU.mult)\
                            .then_inc(dn_uu.sem, 1)
                    for d in range(2):
                        cc = chunk(j, d)
                        need(dn_o, 2 * j + d + 1)
                        for h in range(4):
                            i = 8 * cc + 4 * d + h
                            V.scalar_tensor_tensor(S[d][:, h, :], S[d][:, h, :], cdec[:, i:i + 1],
                                                   bank(4 * d + 1)[:, h * P:(h + 1) * P], ALU.mult, ALU.add)
                        a = cc * P + (DPAD if cc == 4 else 0)
                        out = dnT[:, 8:12, a:a + P]
                        if (d == 0 and j in (0, 1, 4)) or (d == 1 and j < 2):
                            V.tensor_copy(out, heads(bank(4 * d + 3))).then_inc(dn_state.sem, 1)
                        else:
                            need(dn_state, 2 * j + d)
                            V.tensor_tensor(out, out, heads(bank(4 * d + 3)), ALU.add).then_inc(dn_state.sem, 1)
                    if j == 3:
                        need(dn_state, 8)
                        for d in range(2):
                            V.memset(S[d], 0.0).then_inc(ctx_zero.sem, 1)
                        need(ctx_zero, 2)

                parts = ((slice(0, TS), slice(0, TS)), (slice(TS + DPAD, DLEN), slice(TS, T)))
                for h in range(4):
                    need(on_r, h + 1)
                    for a, b in parts:
                        ins = V.scalar_tensor_tensor(dnT[:, 8 + h, a], dnT[:, 8 + h, a], pT[:, R_NG:R_NG + 1], rst[:, b],
                                                     ALU.mult, ALU.mult)
                    step(ins)
                    for a, b in parts:
                        ins = V.tensor_tensor(dnT[:, 8 + h, a], dnT[:, 8 + h, a], zs[:, h, b], ALU.mult)
                    ins.then_inc(mixc_ready.sem, 1)

                def add_to_x(m, s, gain):
                    V.scalar_tensor_tensor(xT[:, m, 0:TS], gslot(s)[:, 0:TS], mod[:, gain + m, 0:1], xT[:, m, 0:TS],
                                           ALU.mult, ALU.add)
                    V.scalar_tensor_tensor(xT[:, m, TS:T], gslot(s)[:, TS:T], mod[:, gain + m, 1:2], xT[:, m, TS:T],
                                           ALU.mult, ALU.add).then_inc(gemm_out[s].sem, 1)

                for m in range(KD):
                    need(gemm_done, G_OUT + m + 1)
                    add_to_x(m, m % 2, 16)
                norm(1)

                def r(a, n):
                    return rt[:, a:a + NCH * n].rearrange("p (c n) -> p c n", c=NCH)

                def wide(ap, n):
                    return ap.rearrange("p (c a) -> p c a", a=1).to_broadcast([P, NCH, n])

                gates, lr, e4, mx, ci, mn = r(0, 16), r(80, 20), r(180, 4), rt[:, 200:205], r(205, 4), rt[:, 225:230]
                og, psum_, ls, o1, o2 = r(230, 4), rt[:, 250:255], r(255, 4), r(275, 4), r(295, 4)
                a1, a2, w1_, l2_, dif, w2_ = rt[:, 315:320], rt[:, 320:325], rt[:, 325:330], r(330, 4), rt[:, 350:355], rt[:, 355:360]
                iota = cst[:, C_IOTA:C_IOTA + 4].rearrange("p (a n) -> p a n", a=1).to_broadcast([P, NCH, 4])

                def one_hot(out, x, best):
                    step(V.tensor_reduce(best, x, AX, ALU.max))
                    step(V.tensor_tensor(ci, x, wide(best, 4), ALU.is_equal))
                    step(V.scalar_tensor_tensor(ci, ci, -8.0, iota, ALU.mult, ALU.add))
                    step(V.tensor_reduce(mn, ci, AX, ALU.min))
                    step(V.tensor_tensor(out, ci, wide(mn, 4), ALU.is_equal))

                need(logits, 1)
                step(V.tensor_tensor(lr, ps[:, 3072:3172].rearrange("p (c n) -> p c n", c=NCH),
                                     rbias.rearrange("p (a n) -> p a n", a=1).to_broadcast([P, NCH, 20]), ALU.add))
                one_hot(og, lr[:, :, 0:4], mx)
                V.tensor_tensor(e4, lr[:, :, 0:4], wide(mx, 4), ALU.subtract).then_inc(rt_in.sem, 1)
                le = lr[:, :, 4:20].rearrange("p c (g e) -> p c g e", g=NG)
                sel = gates.rearrange("p c (g e) -> p c g e", g=NG)
                ogw = og.rearrange("p c (g a) -> p c g a", a=1).to_broadcast([P, NCH, NG, EPG])
                step(V.tensor_tensor(sel, le, ogw, ALU.mult))
                step(V.tensor_reduce(ls, gates.rearrange("p c (g e) -> p c e g", g=NG), AX, ALU.add))
                one_hot(o1, ls, a1)
                step(V.scalar_tensor_tensor(l2_, o1, NEG, ls, ALU.mult, ALU.add))
                one_hot(o2, l2_, a2)
                V.tensor_tensor(dif, a2, a1, ALU.subtract).then_inc(rt_in2.sem, 1)
                need(rt_exp, 1)
                step(V.tensor_reduce(psum_, e4, AX, ALU.add))
                step(V.reciprocal(psum_, psum_))
                need(rt_exp2, 1)
                step(V.tensor_scalar(w1_, dif, 1.0, None, ALU.add))
                step(V.reciprocal(w1_, w1_))
                step(V.tensor_tensor(w1_, w1_, psum_, ALU.mult))
                step(V.tensor_tensor(w2_, dif, w1_, ALU.mult))
                step(V.tensor_tensor(o1, o1, wide(w1_, 4), ALU.mult))
                step(V.tensor_tensor(o2, o2, wide(w2_, 4), ALU.mult))
                step(V.tensor_tensor(o1, o1, o2, ALU.add))
                o1w = o1.rearrange("p c (a e) -> p c a e", a=1).to_broadcast([P, NCH, NG, EPG])
                V.tensor_tensor(sel, ogw, o1w, ALU.mult).then_inc(gates_ready.sem, 1)

                with dve.Fori(0, NE // 2) as pr:
                    def need_pair(sig, n, per):
                        dve.wait_ge(sig.sem, sig.at(l, n) + pr * per)

                    for q in range(2):
                        g0 = G_MOE + 12 * q
                        for f in range(FT):
                            need_pair(gemm_out[0], (g0 + 2 * f) // 2 + 1, G_PAIR // 2)
                            need_pair(gemm_done, g0 + 2 * f + 2, G_PAIR)
                            V.tensor_tensor(mb[f], sil[f], gslot(1), ALU.mult).then_inc(gemm_out[1].sem, 1)
                            need_pair(gemm_out[1], (g0 + 2 * f) // 2 + 1, G_PAIR // 2)
                            need_pair(gate_loaded[q], 16, 16)
                            V.tensor_tensor(hid[2 * q + f], mb[f], gate[q], ALU.mult).then_inc(hid_ready.sem, 1)
                        for m in range(KD):
                            need_pair(gemm_done, g0 + 4 + m + 1, G_PAIR)
                            add_to_x(m, m % 2, 40)

            dve.wait_ge(once["fin_r"], 2)
            for k in range(KD):
                V.scalar_tensor_tensor(xT[:, k, :], xT[:, k, :], pT[:, R_GF + k:R_GF + k + 1], rst, ALU.mult, ALU.mult)\
                    .then_inc(once["fin_y"], 1)
            assert n_step[0] == DVE_STEPS, n_step

        @block.gpsimd
        def _(pool):
            G = nc.gpsimd
            pool.wait_ge(once["cst_loaded"], 16)
            with pool.Fori(0, L) as l:
                def need(sig, n):
                    pool.wait_ge(sig.sem, sig.at(l, n))

                need(bias_loaded, 32)
                slots = tzv[:, 1:, :]

                def rows(a):
                    return cst[:, a:a + GRID].rearrange("p (a n) -> p a n", a=1).to_broadcast([P, NH * RO - 1, GRID])

                G.tensor_tensor(slots, slots, rows(C_COL), ALU.mult).then_inc(pool_step.sem, 1)
                need(pool_step, 1)
                G.tensor_tensor(slots, slots, rows(C_NEG), ALU.add).then_inc(tz_ready.sem, 1)

                for t in range(8):
                    need(l2_x, t + 1)
                    if t >= 2:
                        need(rope_x, t - 1)
                    G.tensor_tensor(rcos[t % 2], dnT[:, t, 0:TS], cst[:, C_COS:C_COS + TS], ALU.mult).then_inc(rope_cos.sem, 1)

                def chunk(j, d):
                    return 4 if j == 4 else (j if d == 0 else 3 - j)

                need(gc_exp, 1)
                need(kv_copied, 8)
                for j in range(5):
                    def block_of(n, d):
                        m = cst[:, C_LEV + (LEV * d + n) * P:C_LEV + (LEV * d + n + 1) * P]
                        G.tensor_tensor(B[d][f"Cs{n % 2}"], B[d]["CT"], over_heads(m), ALU.mult).then_inc(dn_cs.sem, 1)

                    for n in range(2):
                        for d in range(2):
                            need(dn_mat, 2 * j + d + 1)
                            block_of(n, d)
                    for d in range(2):
                        cc = chunk(j, d)
                        a = cc * P + (DPAD if cc == 4 else 0)
                        need(dn_erow, 2 * j + d + 1)
                        G.tensor_tensor(B[d]["qdec"], B[d]["qdec"], dnT[:, 0:4, a:a + P], ALU.mult).then_inc(dn_qk.sem, 1)
                        G.tensor_tensor(B[d]["kdec"], heads(tok[:, 0, cc, :]),
                                        along(ekd[:, 20 * d + 4 * cc:20 * d + 4 * cc + 4], P), ALU.mult).then_inc(dn_qk.sem, 1)
                    for n in range(2, LEV):
                        for d in range(2):
                            if n == 2:
                                need(dn_x, 2 * LEV * j + d + 1)
                            else:
                                need(dn_w, 2 * (LEV - 1) * j + 2 * (n - 3) + d + 1)
                            block_of(n, d)


_INS = ["x_prompt", "x_sample", "cache_na_k", "cache_na_v", "state_delta", "c", "c_ctx", "w_mod", "b_mod", "g_norm1",
        "g_norm2", "w_in", "conv_a_w", "conv_a_b", "ln_a_g", "ln_a_b", "na_rel_bias", "dn_conv_w", "dn_a_log",
        "dn_dt_bias", "dn_norm_g", "w_out", "router_wg", "router_bg", "router_we", "router_be", "w1", "w3", "w2", "g_final"]
_VIEWS = {"cache_na_k": (L, P, NH, HD), "cache_na_v": (L, P, NH, HD), "state_delta": (L, 2, DH, DK, DK),
          "na_rel_bias": (L, NH * RO * CO), "dn_a_log": (L, 8), "dn_dt_bias": (L, 8)}
_OUTS = [("y_prompt", (1, TC, D)), ("y_sample", (1, TS, D)), ("new_k", (L, TC, NH, HD)), ("new_v", (L, TC, NH, HD)),
         ("new_s", (L, 2, DH, DK, DK))]


def kernel(**inputs):
    import concourse.bacc as bacc
    from concourse.bass_utils import run_bass_kernel_spmd

    nc = bacc.Bacc("TRN2", target_bir_lowering=False, num_devices=1)
    arrays, args = {}, []
    for name in [*_INS, "constants"]:
        a = constants() if name == "constants" else np.ascontiguousarray(inputs[name])
        a = a.reshape(_VIEWS.get(name, a.shape))
        arrays[f"in_{name}"] = a
        args.append(nc.dram_tensor(f"in_{name}", a.shape, F32, kind="ExternalInput").ap())
    for name, shape in _OUTS:
        args.append(nc.dram_tensor(f"out_{name}", shape, F32, kind="ExternalOutput").ap())
    build(nc, *args)
    r = run_bass_kernel_spmd(nc, [arrays], core_ids=[0])
    y_prompt, y_sample, new_k, new_v, new_s = (r.results[0][f"out_{name}"] for name, _ in _OUTS)
    return (y_prompt, y_sample, new_k.reshape(1, L, TC, NH, HD), new_v.reshape(1, L, TC, NH, HD),
            new_s.reshape(1, L, 2, DH, DK, DK))
```

```python
from contextlib import ExitStack

import numpy as np
import concourse.bass as bass
from concourse import mybir
from concourse.alu_op_type import AluOpType as ALU

ACT = mybir.ActivationFunctionType
F32 = mybir.dt.float32
AX = mybir.AxisListType.X

P = 128
L = 2
D = 1024
KD = D // P
TS, TC = 512, 128
T = TS + TC
NCH = T // P
GRID = 64
CW, CK = 256, 31
NAW, NH, HD = 256, 4, 64
DNW, DH, DK = 512, 4, 128
DCK = 5
OFF_AB = 2 * CW + 3 * NAW + 3 * DNW + DNW
PROJ = 2 * CW + 3 * NAW + 3 * DNW + DNW + 4 * DH
NE, NG, EPG, FE = 16, 4, 4, 256
FT = FE // P
EPS = 1e-6
NEG = -1e30
CPAD, DPAD = (CK - 1) // 2, (DCK - 1) // 2
CLEN = TS + CPAD + TC
DLEN = TS + DPAD + TC
DST = DLEN + 2
CU, SLEN = CLEN + 2 * CPAD, DLEN + 2 * DPAD
RO, CO = 15, 31
LEV = 7

IN_CHUNKS = [(0, 512), (1280, 512), (1792, 512), (2304, 512), (2816, 512), (512, 512), (1024, 256)]
SLOT = KD * 512
MOD_CHUNKS = [*range(4), *range(11, 19)]
MOD_READ = {i: sum(j % 3 == i % 3 for j in MOD_CHUNKS if j <= i) for i in MOD_CHUNKS}
PRM_DMAS = 17
ACT_STEPS, DVE_STEPS, POOL_STEPS = 17, 222, 1

R_BMOD, R_G1, R_G2, R_CW, R_CB = 0, 48, 56, 64, 126
R_LNG, R_LNB, R_DW, R_NG, R_GF = 128, 130, 132, 192, 193
NROW2 = 201 - 128

G_GLU, G_DN, G_Z, G_QK = 0, 4, 16, 20
G_ATT, G_CTX, G_OUT, G_MOE = 24, 40, 42, 50
G_ALL = G_MOE + KD
NPAIR = ((2 * T + NE * (P - 1)) // P + 1) // 2
NBLK = 2 * NPAIR

C_ID, C_PERM, C_ONE = 0, 128, 256
C_COS, C_SIN = 384, 896
C_UP, C_LO = 1408, 1536
C_LEV = 1664
C_COL = C_LEV + 2 * LEV * P
C_NEG = C_COL + GRID
C_IOTA = C_NEG + GRID
C_SC = C_IOTA + 4
C_THR = C_SC + 4
C_EXC = C_THR + NCH
C_BLK = C_EXC + NE * NE
NC = C_BLK + NBLK


def constants():
    c = np.zeros((P, NC), np.float32)
    i = np.arange(P)
    c[:, C_ID:C_ID + P] = np.eye(P)
    c[i, C_PERM + (i ^ 32)] = 1.0
    c[:, C_ONE:C_ONE + P] = 1.0
    pos = np.arange(TS)
    nf = DK // 4
    inv = 10000.0 ** (-np.arange(nf) / nf)
    for d in range(P):
        ang = (pos // GRID if d < 64 else pos % GRID) * inv[d % 32]
        c[d, C_COS:C_COS + TS] = np.cos(ang)
        c[d, C_SIN:C_SIN + TS] = np.sin(ang) * (-1.0 if d % 64 < 32 else 1.0)
    a, b = i[:, None], i[None, :]
    c[:, C_UP:C_UP + P] = a <= b
    c[:, C_LO:C_LO + P] = a >= b
    for n in range(LEV):
        s = 1 << n
        fw = (a // (2 * s) == b // (2 * s)) & (b // s == a // s + 1)
        c[:, C_LEV + n * P:C_LEV + (n + 1) * P] = fw
        c[:, C_LEV + (LEV + n) * P:C_LEV + (LEV + n + 1) * P] = fw.T
    q, k = (i % GRID)[:, None], np.arange(GRID)[None, :]
    cs = np.clip(q - 8, 0, GRID - 16)
    c[:, C_COL:C_COL + GRID] = (k >= cs) & (k < cs + 16)
    c[:, C_NEG:C_NEG + GRID] = NEG * (1.0 - c[:, C_COL:C_COL + GRID])
    c[:, C_IOTA:C_IOTA + 4] = np.arange(4)
    c[:, C_SC] = EPS
    c[:, C_SC + 1] = -0.5 * np.log(DK)
    c[:, C_SC + 2] = 1.0
    c[:, C_THR:C_THR + NCH] = P * np.arange(NCH)
    e = np.arange(NE)
    c[:, C_EXC:C_EXC + NE * NE] = (e[None, :] < e[:, None]).reshape(-1)
    c[:, C_BLK:C_BLK + NBLK] = np.arange(NBLK)
    return c


class Signal:

    def __init__(self, sem, per_layer, first=0):
        self.sem, self.per_layer, self.first = sem, per_layer, first

    def at(self, layer, n):
        return layer * self.per_layer + (n + self.first)


def build(nc, x_prompt, x_sample, cache_k, cache_v, state, c, c_ctx, w_mod, b_mod, g1, g2, w_in, conv_w,
          conv_b, ln_g, ln_b, rel_bias, dn_conv_w, a_log, dt_bias, norm_g, w_out, wg, bg, we, be, w1, w3, w2,
          g_final, consts, y_prompt, y_sample, new_k, new_v, new_s, dbg=None):
    BP = GRID + NH * RO * CO + GRID
    bias_pad = nc.dram_tensor("bias_pad", (GRID, BP), F32, kind="Internal")
    xs = nc.dram_tensor("xs", ((NBLK + 1) * P, D), F32, kind="Internal").ap()
    ys = nc.dram_tensor("ys", (NBLK * P, D), F32, kind="Internal").ap()
    NB = NH * RO * CO

    with ExitStack() as ctx:
        def sb(name, shape):
            return ctx.enter_context(nc.sbuf_tensor(name, shape, F32))

        def signal(name, per_layer, first=0):
            return Signal(ctx.enter_context(nc.semaphore(name)), per_layer, first)

        def heads(ap):
            return ap.rearrange("p (h n) -> p h n", h=4)

        ps = ctx.enter_context(nc.psum_tensor("ps", [P, 8 * 512], F32))
        ring = [sb(f"ring{i}", [P, SLOT]) for i in range(3)]
        xT = sb("xT", [P, KD, T])
        hreg = sb("hreg", [P, KD * T])
        hT = hreg[:, :].rearrange("p (k t) -> p k t", k=KD)
        dnT = sb("dnT", [P, 12, DST])
        tok = sb("tok", [P, 2, NCH, DH * DK])
        zs = sb("zs", [P, DH, T])
        mixA = sb("mixA", [P, 2, CLEN])
        mixb_reg = sb("mixb_reg", [P, 2 * SLEN])
        mixB = mixb_reg[:, 0:2 * T].rearrange("p (t n) -> p t n", t=2)
        stage = [mixb_reg[:, SLEN * i:SLEN * (i + 1)] for i in range(2)]
        cst = sb("cst", [P, NC])
        work = sb("work", [P, 6 * T])
        small = sb("small", [P, 1110])
        rst = sb("rst", [P, T])[:, :]
        tmp_reg = sb("tmp_reg", [P, 2 * CLEN])
        tmp = tmp_reg[:, :].rearrange("p (t n) -> p t n", t=2)
        prm = tmp_reg[:, 0:2 * P].rearrange("p (t n) -> p t n", t=2)
        cin_reg = sb("cin_reg", [P, 2 * CU])
        cin = cin_reg[:, :].rearrange("p (t n) -> p t n", t=2)
        S = [heads(cin_reg[:, 512 * d:512 * d + 512]) for d in range(2)]
        qkT = work[:, 0:4 * T].rearrange("p (t n) -> p t n", t=4)
        vna = work[:, 4 * T:4 * T + NCH * NAW].rearrange("p (t n) -> p t n", t=NCH)
        mrow = [work[0:2, 512 * i:512 * i + 512] for i in range(4)]
        lrow = work[0:20, 2048:2048 + T]
        at = [0]

        def carve(n):
            at[0] += n
            return small[:, at[0] - n:at[0]]

        pT = carve(201)
        condT = carve(2 * KD)
        mod = carve(96).rearrange("p (j c) -> p j c", c=2)
        A = [carve(2 * KD).rearrange("p (j c) -> p j c", c=2) for _ in range(2)]
        alog, dtb, ealog = carve(8), carve(8), carve(8)
        rbias = carve(20)
        wr = carve(KD * 20).rearrange("p (k n) -> p k n", k=KD)
        wab = carve(KD * 16).rearrange("p (k n) -> p k n", k=KD)
        st = carve(16)
        rt = small[:, at[0]:at[0] + 400]
        ab = carve(80).rearrange("p (c n) -> p c n", c=NCH)
        gsp = carve(40).rearrange("p (c n) -> p c n", c=NCH)
        gt1 = carve(40).rearrange("p (c n) -> p c n", c=NCH)
        beta = carve(40).rearrange("p (c n) -> p c n", c=NCH)
        gcum = carve(80)
        egc = carve(40)
        ekd = carve(40)
        cdec = carve(40)

        def gslot(s):
            return ps[:, 1024 * s:1024 * s + T]

        def bank(b, n=512):
            return ps[:, 512 * b:512 * b + n]

        ident = cst[:, C_ID:C_ID + P]
        ones = cst[:, C_ONE:C_ONE + P]
        eps_c, lnsc_c, one_c = (cst[:, C_SC + i:C_SC + i + 1] for i in range(3))

        def over_heads(ap):
            return ap.rearrange("p (a n) -> p a n", a=1).to_broadcast([P, 4, ap.shape[-1]])

        def along(ap, n):
            return ap.rearrange("p (h a) -> p h a", a=1).to_broadcast([P, ap.shape[-1], n])

        names = ["DT", "CT", "aqk", "Cs0", "X", "XT", "W", "qdec", "kdec"]
        places = [[hreg[:, 512 * i:512 * i + 512] for i in range(9)],
                  [work[:, 512 * i:512 * i + 512] for i in range(7)] + [tmp_reg[:, 0:512], tmp_reg[:, 512:1024]]]
        B = [{n: heads(r) for n, r in zip(names, regs)} for regs in places]
        for b_ in B:
            b_["Cs1"] = b_["DT"]
        sc = [hreg[:, 640 * i:640 * i + 640] for i in range(2)]
        pT_ = [hreg[:, 640 * (2 + i):640 * (3 + i)] for i in range(2)]
        kvc = [hreg[:, 2560 + 256 * i:2816 + 256 * i] for i in range(2)]
        kcT = hreg[:, 3072:3328]
        newk = hreg[:, 3328:3584]
        rcos = [hreg[:, 3584 + 512 * i:4096 + 512 * i] for i in range(2)]
        rsin = hreg[:, 4608:5120]
        Tz = tok[:, :, :, :].rearrange("p a c n -> p (a c n)")[:, 0:NH * RO * GRID]
        tzv = Tz.rearrange("p (a n) -> p a n", n=GRID)
        dflat = dnT[:, :, :].rearrange("p a b -> p (a b)")
        htok = dflat[:, 0:NCH * D].rearrange("p (c d) -> p c d", c=NCH)
        tflat = tok[:, :, :, :].rearrange("p a c n -> p (a c n)")
        zflat = zs[:, :, :].rearrange("p a b -> p (a b)")
        xg = [tflat[:, D * i:D * (i + 1)] for i in range(2)]
        xgT = [tflat[:, D * (2 + i):D * (3 + i)].rearrange("p (k n) -> p k n", k=KD) for i in range(2)]
        ysb = [zflat[:, D * i:D * (i + 1)] for i in range(2)]
        sil, hid = work[:, 0:FE], work[:, FE:2 * FE]
        hidT = work[:, 2 * FE:3 * FE]
        rsc = work[:, 1024:2048]
        yg = [hreg[:, 2 * D * i:2 * D * (i + 1)].rearrange("p (i d) -> p i d", i=2) for i in range(2)]
        slots = ctx.enter_context(nc.sbuf_tensor("slots", [P, 2 * NCH], mybir.dt.uint32))
        blocks = ctx.enter_context(nc.sbuf_tensor("blocks", [P, NBLK + 1], mybir.dt.int32))
        zero = sb("zero", [P, P])
        xload = hreg[:, :].rearrange("p (c d) -> p c d", c=NCH)

        once = {n: ctx.enter_context(nc.semaphore(n)) for n in
                ("first_loaded", "x_turned", "cond_ready", "pad_ready", "pads_written", "cst_loaded", "y_turned", "y_copied",
                 "y_stored", "pool_turns", "sp_turns", "pe_turns", "act_turns",
                 "dve_turns", "cond_turned", "fin_sq", "fin_ss", "fin_r", "fin_y", "pe_first")}
        ring_loaded = [signal(f"ring_loaded{i}", 16 * 7 + 32 * n) for i, n in enumerate((NPAIR, NPAIR, 0))]
        w2_loaded = [signal(f"w2_loaded{i}", 16 * NPAIR) for i in range(2)]
        mod_used = [signal(f"mod_used{i}", n) for i, n in enumerate((5, 3, 4))]
        gemm_done = signal("gemm_done", G_ALL, 1)
        gemm_out = [signal(f"gemm_out{i}", G_ALL // 2, 1) for i in range(2)]
        prm_loaded = signal("prm_loaded", 16 * PRM_DMAS)
        bias_copied = signal("bias_copied", 16)
        bias_loaded = signal("bias_loaded", 32)
        kvc_loaded = signal("kvc_loaded", 32)
        state_loaded = signal("state_loaded", 32)
        prm_turned = signal("prm_turned", 1)
        pT_ready = signal("pT_ready", 1)
        mod_copied = signal("mod_copied", 12)
        mod_turned = signal("mod_turned", 12)
        mod_ready = signal("mod_ready", 1)
        mod2_ready = signal("mod2_ready", 1)
        sq_ready = signal("sq_ready", 2 * KD)
        norm_ss = signal("norm_ss", 2)
        norm_r = signal("norm_r", 2)
        norm_x = signal("norm_x", 2 * KD)
        h_ready = signal("h_ready", 2 * KD)
        dn_conv = signal("dn_conv", 12)
        dn_silu = signal("dn_silu", 12)
        ab_done = signal("ab_done", 1)
        ab_copied = signal("ab_copied", 1)
        v_done = signal("v_done", 1)
        v_copied = signal("v_copied", 1)
        conv_out = signal("conv_out", 1)
        ln_sum = signal("ln_sum", 1)
        ln_xc = signal("ln_xc", 2)
        ln_sq = signal("ln_sq", 2)
        ln_var = signal("ln_var", 1)
        ln_r = signal("ln_r", 1)
        ln_y = signal("ln_y", 2)
        mixa_ready = signal("mixa_ready", 2)
        kc_turned = signal("kc_turned", 1)
        kc_copied = signal("kc_copied", 1)
        newk_turned = signal("newk_turned", 1)
        newk_copied = signal("newk_copied", 1)
        newkv_stored = signal("newkv_stored", 32)
        tz_ready = signal("tz_ready", 1)
        att_s = signal("att_s", 18)
        att_p = signal("att_p", 18)
        att_n = signal("att_n", 18)
        att_pt = signal("att_pt", 18)
        att_ptc = signal("att_ptc", 18)
        att_o = signal("att_o", 20)
        att_oc = signal("att_oc", 20)
        l2_sq = signal("l2_sq", 8)
        l2_ss = signal("l2_ss", 8)
        l2_r = signal("l2_r", 8)
        l2_x = signal("l2_x", 8)
        rope_mm = signal("rope_mm", 8)
        rope_cos = signal("rope_cos", 8)
        rope_x = signal("rope_x", 8)
        kv_turned = signal("kv_turned", 8)
        kv_copied = signal("kv_copied", 8)
        ctx_zero = signal("ctx_zero", 2)
        pads_zeroed = signal("pads_zeroed", 1)
        conv_in = signal("conv_in", 2)
        beta_tanh = signal("beta_tanh", 1)
        g_abs = signal("g_abs", 1)
        g_act = signal("g_act", 1)
        g_ready = signal("g_ready", 1)
        gc_done = signal("gc_done", 1)
        gc_copied = signal("gc_copied", 1)
        gc_exp = signal("gc_exp", 1)
        dn_row = signal("dn_row", 10)
        dn_gram = signal("dn_gram", 10)
        dn_erow = signal("dn_erow", 10)
        dn_dlog = signal("dn_dlog", 10)
        dn_dexp = signal("dn_dexp", 10)
        dn_mat = signal("dn_mat", 10)
        dn_aqk = signal("dn_aqk", 10)
        dn_cs = signal("dn_cs", 10 * LEV)
        dn_qk = signal("dn_qk", 20)
        dn_c1 = signal("dn_c1", 10)
        dn_x = signal("dn_x", 10 * LEV)
        dn_w = signal("dn_w", 10 * (LEV - 1))
        dn_wc = signal("dn_wc", 10 * (LEV - 1))
        dn_y = signal("dn_y", 10 * (LEV - 1))
        dn_ks = signal("dn_ks", 10)
        dn_res = signal("dn_res", 10)
        dn_u = signal("dn_u", 10)
        dn_uu = signal("dn_uu", 10)
        dn_o = signal("dn_o", 10)
        dn_state = signal("dn_state", 10)
        state_stored = signal("state_stored", 32)
        on_sq = signal("on_sq", 4)
        on_ss = signal("on_ss", 4)
        on_r = signal("on_r", 4)
        mixc_ready = signal("mixc_ready", 4)
        logit_rows = signal("logit_rows", 1)
        logit_copied = signal("logit_copied", 1)
        logits = signal("logits", 1)
        rt_in = signal("rt_in", 1)
        rt_exp = signal("rt_exp", 1)
        rt_in2 = signal("rt_in2", 1)
        rt_exp2 = signal("rt_exp2", 1)
        sel_ready = signal("sel_ready", 1)
        ranks = signal("ranks", 1)
        slots_ready = signal("slots_ready", 1)
        blocks_ready = signal("blocks_ready", 1)
        ht_turned = signal("ht_turned", NCH)
        ht_copied = signal("ht_copied", NCH)
        xys_zeroed = ctx.enter_context(nc.semaphore("xys_zeroed"))
        xs_written = signal("xs_written", 16 * 2 * NCH)
        xg_loaded = [signal(f"xg_loaded{i}", 16 * (NPAIR + 1 - i)) for i in range(2)]
        xg_turned = signal("xg_turned", NBLK + 1, 2)
        xg_copied = signal("xg_copied", NBLK + 1)
        up_done = signal("up_done", NBLK, 2)
        sil_ready = signal("sil_ready", NBLK)
        hid_ready = signal("hid_ready", NBLK)
        hid_turned = signal("hid_turned", NBLK)
        hid_copied = signal("hid_copied", NBLK)
        y_done = signal("y_done", NBLK, 2)
        y_out = signal("y_out", NBLK, 2)
        ys_stored = [signal(f"ys_stored{i}", 16 * NPAIR, 16) for i in range(2)]
        yg_loaded = [signal(f"yg_loaded{i}", 32 * n) for i, n in enumerate((3, 2))]
        comb_done = signal("comb_done", NCH)
        act_step = signal("act_step", ACT_STEPS)
        dve_step = signal("dve_step", DVE_STEPS)
        pool_step = signal("pool_step", POOL_STEPS)

        block = ctx.enter_context(nc.Block())

        @block.sync
        def _(sp):
            sp.dma_start(cst[:, :], consts).then_inc(once["cst_loaded"], 16)
            sp.dma_start(xload[:, 0:4, :], x_sample[0].rearrange("(c p) d -> p c d", p=P)).then_inc(once["first_loaded"], 16)
            sp.dma_start(xload[:, 4, :], x_prompt[0]).then_inc(once["first_loaded"], 16)
            sp.dma_start(prm[0:8, 0, :], c[0].rearrange("(k p) -> k p", p=P)).then_inc(once["first_loaded"], 16)
            sp.dma_start(prm[8:16, 0, :], c_ctx.rearrange("(k p) -> k p", p=P)).then_inc(once["first_loaded"], 16)
            sp.wait_ge(once["pad_ready"], 1)
            for o in (0, GRID + NB):
                sp.dma_start(bias_pad.ap()[:, o:o + GRID], rst[0:GRID, 0:GRID]).then_inc(once["pads_written"], 16)
            with sp.Fori(0, L) as l:
                def need(sig, n):
                    sp.wait_ge(sig.sem, sig.at(l, n))

                for i in range(21):
                    s = i % 3
                    if i < 2:
                        need(up_done, 0)
                    elif i == 2:
                        need(y_done, 0)
                    elif i < 7:
                        need(mod_used[s], MOD_READ[i - 3])
                    elif i < 11:
                        need(gemm_done, 4 * (i - 6))
                    elif i < 13:
                        need(gemm_done, G_Z + 4 * (i - 10))
                    elif i == 13:
                        need(v_done, 1)
                    else:
                        need(mod_used[s], MOD_READ[i - 3])
                    if i < 4 or 11 <= i < 19:
                        c_ = i if i < 4 else i - 7
                        src, w = w_mod[l][:, 512 * c_:512 * c_ + 512], 512
                    elif i < 11:
                        o, w = IN_CHUNKS[i - 4]
                        src = w_in[l][:, o:o + w]
                    else:
                        src, w = w_out[l][:, 512 * (i - 19):512 * (i - 18)], 512
                    dst = ring[s][:, 0:KD * w].rearrange("p (k n) -> p k n", k=KD)
                    sp.dma_start(dst, src.rearrange("(k p) n -> p k n", p=P)).then_inc(ring_loaded[s].sem, 16)

                def up_load(q, e):
                    dst = ring[q][:, :].rearrange("p (k m n) -> p m k n", k=KD, m=2)
                    for m, w in enumerate((w1, w3)):
                        sp.dma_start(dst[:, m], w[l, e].rearrange("(k p) n -> p k n", p=P)).then_inc(ring_loaded[q].sem, 16)

                def down_load(q, e):
                    dst = ring[2][:, 2048 * q:2048 * q + 2048].rearrange("p (k n) -> p k n", k=FT)
                    sp.dma_start(dst, w2[l, e].rearrange("(k p) n -> p k n", p=P)).then_inc(w2_loaded[q].sem, 16)

                def xg_load(q, b):
                    sp.dma_start(xg[q], xs[bass.ds(b * P, P), :]).then_inc(xg_loaded[q].sem, 16)

                need(mod_used[0], MOD_READ[18])
                up_load(0, 0)
                need(gemm_done, G_OUT + 8)
                down_load(0, 0)
                need(blocks_ready, 1)
                sp.sem_inc(once["sp_turns"], 1)
                e = sp.value_load(blocks[0:1, 1:2], min_val=0, max_val=NE - 1)
                up_load(1, e)
                down_load(1, e)
                need(xs_written, 16 * 2 * NCH)
                xg_load(0, 0)
                xg_load(1, 1)
                need(xg_turned, 1)
                xg_load(0, 2)
                in_use = sp.value_load(blocks[0:1, NBLK:NBLK + 1], min_val=1, max_val=NBLK)
                with sp.Fori(1, NPAIR) as pr:
                    with sp.If(pr * 2 < in_use):
                        for q in range(2):
                            e = sp.value_load(blocks[0:1, bass.ds(pr * 2 + q, 1)], min_val=0, max_val=NE - 1)
                            sp.wait_ge(up_done.sem, up_done.at(l, q - 1) + pr * 2)
                            up_load(q, e)
                            sp.wait_ge(xg_turned.sem, xg_turned.at(l, q) + pr * 2)
                            xg_load(1 - q, pr * 2 + q + 1)
                            sp.wait_ge(y_done.sem, y_done.at(l, q - 1) + pr * 2)
                            down_load(q, e)
                    with sp.Else():
                        for q in range(2):
                            sp.wait_ge(ring_loaded[q].sem, ring_loaded[q].at(l, 16 * 7) + pr * 32)
                            sp.sem_inc(ring_loaded[q].sem, 32)
                            sp.wait_ge(w2_loaded[q].sem, w2_loaded[q].at(l, 0) + pr * 16)
                            sp.sem_inc(w2_loaded[q].sem, 16)
                            sp.wait_ge(xg_loaded[q].sem, xg_loaded[q].at(l, 16 * (1 - q)) + pr * 16)
                            sp.sem_inc(xg_loaded[q].sem, 16)
            sp.wait_ge(once["y_stored"], 32)

        @block.tensor
        def _(pe):
            mm = nc.tensor.matmul
            turn = nc.tensor.transpose

            pe.sem_inc(gemm_done.sem, 1)
            for s in (xg_turned, up_done, y_done):
                pe.sem_inc(s.sem, 2)
            pe.wait_ge(once["cst_loaded"], 16)
            pe.wait_ge(once["first_loaded"], 64)
            for k in range(KD):
                if k >= 2:
                    pe.wait_ge(once["x_turned"], k - 1)
                for t in range(NCH):
                    ins = turn(gslot(k % 2)[:, t * P:(t + 1) * P], xload[:, t, k * P:(k + 1) * P], ident)
                ins.then_inc(once["pe_first"], 1)
            turn(bank(4, 16), prm[0:16, 0, :], ident[0:16, 0:16]).then_inc(once["cond_turned"], 1)
            pe.wait_ge(once["x_turned"], KD)
            pe.wait_ge(once["cond_ready"], 1)

            with pe.Fori(0, L) as l:
                def need(sig, n):
                    pe.wait_ge(sig.sem, sig.at(l, n))

                ct = condT.rearrange("p (c k) -> p c k", c=2)

                def mod_rows(m, bnk):
                    i = MOD_CHUNKS[m]
                    need(ring_loaded[i % 3], 16 * (i // 3 + 1))
                    w = ring[i % 3][:, 0:4096].rearrange("p (k n) -> p k n", k=KD)
                    for k in range(KD):
                        ins = mm(bank(bnk)[0:2], ct[:, :, k], w[:, k, :], start=k == 0, stop=k == KD - 1)
                    ins.then_inc(mod_used[i % 3].sem, 1)

                def mod_turn(m, at_):
                    need(mod_copied, m + 1)
                    pe.sem_inc(once["pe_turns"], 1)
                    for j in range(4):
                        ins = turn(ps[:, at_ + 2 * j:at_ + 2 * j + 2], mrow[m % 4][:, P * j:P * (j + 1)], ident[0:2, 0:2])
                    ins.then_inc(mod_turned.sem, 1)

                for m in range(4):
                    if m >= 2:
                        need(mod_copied, m - 1)
                    mod_rows(m, 4 + m % 2)
                    if m:
                        mod_turn(m - 1, 3072 + 8 * (m - 1))
                mod_turn(3, 3072 + 24)
                need(prm_loaded, 16 * PRM_DMAS)
                turn(bank(7, P), prm[:, 0, :], ident)
                turn(ps[:, 3584 + P:3584 + P + NROW2], prm[0:NROW2, 1, :], ident[0:NROW2, 0:NROW2]).then_inc(prm_turned.sem, 1)

                def norm_sums(n):
                    need(mod_ready, 1)
                    for k in range(KD):
                        need(sq_ready, n * KD + k + 1)
                        mm(bank(4), ones, hT[:, k, 0:TS], start=k == 0, stop=k == KD - 1)
                        ins = mm(bank(5, TC), ones, hT[:, k, TS:T], start=k == 0, stop=k == KD - 1)
                    ins.then_inc(norm_ss.sem, 1)

                def gemm(g, lhs, rhs, nk=KD, before=None):
                    need(gemm_out[g % 2], g // 2)
                    o = gslot(g % 2)
                    for k in range(nk):
                        if before:
                            before(k)
                        mm(o[:, 0:TS], lhs(k), rhs(k)[:, 0:TS], start=k == 0, stop=k == nk - 1)
                        ins = mm(o[:, TS:T], lhs(k), rhs(k)[:, TS:T], start=k == 0, stop=k == nk - 1)
                    ins.then_inc(gemm_done.sem, 1)

                norm_sums(0)
                g = 0
                for ci, (o, w) in enumerate(IN_CHUNKS):
                    s = (4 + ci) % 3
                    need(ring_loaded[s], 16 * ((4 + ci) // 3 + 1))
                    wt = ring[s][:, 0:KD * w].rearrange("p (k n) -> p k n", k=KD)
                    if w == 256:
                        for t in range(NCH):
                            for k in range(KD):
                                ins = mm(ps[:, 2048 + 256 * t:2304 + 256 * t], hT[:, k, t * P:(t + 1) * P], wt[:, k, :],
                                         start=k == 0, stop=k == KD - 1)
                        ins.then_inc(v_done.sem, 1)
                        continue
                    for m in range(4):
                        gemm(g, lambda k: wt[:, k, m * P:(m + 1) * P], lambda k: hT[:, k, :],
                             before=(lambda k: need(h_ready, k + 1)) if g == 0 else None)
                        g += 1
                    if ci == 4:
                        need(pT_ready, 1)
                        for t in range(NCH):
                            for k in range(KD):
                                ins = mm(ps[:, 3584 + 16 * t:3600 + 16 * t], hT[:, k, t * P:(t + 1) * P], wab[:, k, :],
                                         start=k == 0, stop=k == KD - 1)
                        ins.then_inc(ab_done.sem, 1)

                need(v_copied, 1)
                need(conv_out, 1)
                need(ab_copied, 1)
                need(beta_tanh, 1)
                for t in range(2):
                    mm(bank(6), ones, mixA[:, t, 0:TS], start=t == 0, stop=t == 1)
                    ins = mm(bank(7, TC), ones, mixA[:, t, TS + CPAD:CLEN], start=t == 0, stop=t == 1)
                ins.then_inc(ln_sum.sem, 1)

                need(kvc_loaded, 32)
                for t in range(2):
                    ins = turn(ps[:, 2048 + P * t:2048 + P * (t + 1)], kvc[0][:, P * t:P * (t + 1)], ident)
                ins.then_inc(kc_turned.sem, 1)
                need(gemm_out[1], G_ATT // 2)
                need(gemm_out[0], G_ATT // 2)
                for t in range(2):
                    ins = turn(ps[:, 2560 + P * t:2560 + P * (t + 1)], qkT[:, 2 + t, TS:T], ident)
                ins.then_inc(newk_turned.sem, 1)

                for t in range(2):
                    need(ln_sq, 2)
                    mm(bank(6), ones, tmp[:, t, 0:TS], start=t == 0, stop=t == 1)
                    ins = mm(bank(7, TC), ones, tmp[:, t, TS + CPAD:CLEN], start=t == 0, stop=t == 1)
                ins.then_inc(ln_var.sem, 1)

                def scores(i):
                    gg = G_ATT + i
                    need(gemm_out[gg % 2], gg // 2)
                    o = gslot(gg % 2)
                    if i < 16:
                        t, h = i // 4, i % 4
                        r = slice(64 * (h % 2), 64 * (h % 2) + 64)
                        qa = qkT[r, h // 2, t * P:(t + 1) * P]
                        mm(o[:, 0:TS], qa, qkT[r, 2 + h // 2, 0:TS], start=True, stop=True)
                        ins = mm(o[:, TS:T], qa, kcT[r, P * (h // 2):P * (h // 2 + 1)], start=True, stop=True)
                    else:
                        for j in range(2):
                            r = slice(64 * j, 64 * j + 64)
                            ins = mm(o[:, TS * j:TS * j + P], qkT[r, i - 16, TS:T], qkT[r, 2 + i - 16, TS:T],
                                     start=True, stop=True)
                    ins.then_inc(gemm_done.sem, 1)

                def turn_probs(i):
                    need(att_n, i + 1)
                    if i >= 1:
                        need(att_ptc, i)
                    for j in range(NCH if i < 16 else 2):
                        ins = turn(ps[:, 2048 + P * j:2048 + P * (j + 1)], sc[i % 2][:, P * j:P * (j + 1)], ident)
                    ins.then_inc(att_pt.sem, 1)

                def values(i):
                    need(att_ptc, i + 1)
                    src = pT_[i % 2]
                    for h in ([i % 4] if i < 16 else [2 * (i - 16), 2 * (i - 16) + 1]):
                        u = i if i < 16 else h + 16
                        r = slice(64 * (h % 2), 64 * (h % 2) + 64)
                        o = ps[r, 512 * (6 + u % 2):512 * (6 + u % 2) + P]
                        if u >= 2:
                            need(att_oc, u - 1)
                        if i < 16:
                            for j in range(NCH):
                                va = vna[:, j, 64 * h:64 * h + 64] if j < 4 else kvc[1][:, 64 * h:64 * h + 64]
                                ins = mm(o, va, src[:, P * j:P * (j + 1)], start=j == 0, stop=j == NCH - 1)
                        else:
                            ins = mm(o, vna[:, 4, 64 * h:64 * h + 64], src[:, P * (h % 2):P * (h % 2 + 1)], start=True, stop=True)
                        ins.then_inc(att_o.sem, 1)

                need(kc_copied, 1)
                need(newk_copied, 1)
                need(ln_r, 1)
                scores(0)
                scores(1)
                for i in range(18):
                    turn_probs(i)
                    if i + 2 < 18:
                        scores(i + 2)
                    values(i)

                def l2_sums(t):
                    need(l2_sq, t + 1)
                    a = 2048 + 1024 * (t % 2)
                    mm(ps[:, a:a + TS], ones, tmp[:, t % 2, 0:TS], start=True, stop=True)
                    mm(ps[:, a + TS:a + T], ones, tmp[:, t % 2, TS + DPAD:DLEN], start=True, stop=True).then_inc(l2_ss.sem, 1)

                def rope(t):
                    need(l2_x, t + 1)
                    if t >= 2:
                        need(rope_x, t - 1)
                    mm(bank(2 * (t % 2)), cst[:, C_PERM:C_PERM + P], dnT[:, t, 0:TS], start=True, stop=True)\
                        .then_inc(rope_mm.sem, 1)

                need(att_ptc, 18)
                need(att_oc, 20)
                need(gemm_out[0], (G_CTX + 2) // 2)
                need(gemm_out[1], (G_CTX + 2) // 2)
                for t in range(9):
                    if t < 8:
                        l2_sums(t)
                    if t >= 1:
                        rope(t - 1)
                    if t >= 1:
                        mod_turn(3 + t, 1536 + 8 * (t - 1))
                    if t < 8:
                        mod_rows(4 + t, 1)

                for t in range(8):
                    if t < 4:
                        need(rope_x, 4 + t + 1)
                    if t < 2:
                        need(l2_r, 8)
                    else:
                        need(kv_copied, t - 1)
                    for j in range(NCH):
                        a = j * P + (DPAD if j == 4 else 0)
                        ins = turn(ps[:, 2048 + 1024 * (t % 2) + P * j:2048 + 1024 * (t % 2) + P * (j + 1)],
                                   dnT[:, 4 + t, a:a + P], ident)
                    ins.then_inc(kv_turned.sem, 1)
                need(g_ready, 1)
                need(rope_x, 8)
                mm(ps[:, 0:20], cst[:, C_UP:C_UP + P], gsp[:, :, 0:4], start=True, stop=True)
                mm(ps[:, 20:40], cst[:, C_LO:C_LO + P], gsp[:, :, 4:8], start=True, stop=True)
                mm(ps[:, 40:80], ones, gsp[:, :, :], start=True, stop=True).then_inc(gc_done.sem, 1)

                def chunk(j, d):
                    return 4 if j == 4 else (j if d == 0 else 3 - j)

                def cols(cc):
                    a = cc * P + (DPAD if cc == 4 else 0)
                    return slice(a, a + P)

                need(kv_copied, 8)
                need(gc_exp, 1)
                need(mod2_ready, 1)

                def decay_rows(j):
                    for d in range(2):
                        tri = cst[:, (C_UP, C_LO)[d]:(C_UP, C_LO)[d] + P]
                        for h in range(4):
                            gate = gsp[:, chunk(j, d), 4 * d + h:4 * d + h + 1]
                            ins = mm(bank(4 * d)[:, h * P:(h + 1) * P], gate.to_broadcast([P, P]), tri, start=True, stop=True)
                        ins.then_inc(dn_row.sem, 1)

                decay_rows(0)
                for j in range(5):
                    for d in range(2):
                        u = 2 * j + d
                        cc = chunk(j, d)
                        b0 = 4 * d
                        if j:
                            need(dn_state, u - 1)
                        for h in range(4):
                            kk = dnT[:, 4 + h, cols(cc)]
                            mm(bank(b0 + 1)[:, h * P:(h + 1) * P], kk, kk, start=True, stop=True)
                        for h in range(4):
                            kk = dnT[:, 4 + h, cols(cc)]
                            ins = mm(bank(b0 + 2)[:, h * P:(h + 1) * P], kk, dnT[:, h, cols(cc)], start=True, stop=True)
                        ins.then_inc(dn_gram.sem, 1)
                    for d in range(2):
                        u = 2 * j + d
                        need(dn_cs, u // 2 * 2 * LEV + d + 1)
                        need(dn_erow, u + 1)
                        for h in range(4):
                            ins = turn(bank(4 * d)[:, h * P:(h + 1) * P], B[d]["Cs0"][:, h, :], ident)
                        ins.then_inc(dn_c1.sem, 1)
                    for n in range(1, LEV):
                        for d in range(2):
                            need(dn_x, 2 * LEV * j + 2 * (n - 1) + d + 1)
                            need(dn_cs, 2 * LEV * j + 2 * n + d + 1)
                            for h in range(4):
                                ins = mm(bank(4 * d)[:, h * P:(h + 1) * P], B[d][f"Cs{n % 2}"][:, h, :], B[d]["X"][:, h, :],
                                         start=True, stop=True)
                            ins.then_inc(dn_w.sem, 1)
                        for d in range(2):
                            need(dn_wc, 2 * (LEV - 1) * j + 2 * (n - 1) + d + 1)
                            for h in range(4):
                                if n < LEV - 1:
                                    mm(bank(4 * d + 1)[:, h * P:(h + 1) * P], B[d]["XT"][:, h, :], B[d]["W"][:, h, :],
                                       start=True, stop=True)
                            for h in range(4):
                                ins = mm(bank(4 * d + 2)[:, h * P:(h + 1) * P], B[d]["W"][:, h, :], B[d]["XT"][:, h, :],
                                         start=True, stop=True)
                            ins.then_inc(dn_y.sem, 1)
                    for d in range(2):
                        cc = chunk(j, d)
                        if j == 0:
                            need(state_loaded, 32)
                        else:
                            need(dn_state, 2 * j)
                        if j == 4:
                            need(ctx_zero, d + 1)
                        need(dn_x, 2 * LEV * (j + 1) - 1 + d)
                        for h in range(4):
                            ins = mm(bank(4 * d + 1)[:, h * P:(h + 1) * P], dnT[:, 4 + h, cols(cc)], S[d][:, h, :],
                                     start=True, stop=True)
                        ins.then_inc(dn_ks.sem, 1)
                    if j < 4:
                        decay_rows(j + 1)
                    for d in range(2):
                        need(dn_res, 2 * j + d + 1)
                        for h in range(4):
                            ins = mm(bank(4 * d + 2)[:, h * P:(h + 1) * P], B[d]["XT"][:, h, :], B[d]["CT"][:, h, :],
                                     start=True, stop=True)
                        ins.then_inc(dn_u.sem, 1)
                    for d in range(2):
                        need(dn_uu, 2 * j + d + 1)
                        need(dn_qk, 4 * j + 2 * d + 2)
                        for h in range(4):
                            o = bank(4 * d + 3)[:, h * P:(h + 1) * P]
                            mm(o, S[d][:, h, :], B[d]["qdec"][:, h, :], start=True, stop=False)
                            mm(o, B[d]["W"][:, h, :], B[d]["aqk"][:, h, :], start=False, stop=True)
                        for h in range(4):
                            ins = mm(bank(4 * d + 1)[:, h * P:(h + 1) * P], B[d]["kdec"][:, h, :], B[d]["W"][:, h, :],
                                     start=True, stop=True)
                        ins.then_inc(dn_o.sem, 1)

                need(dn_state, 10)
                for h in range(4):
                    need(on_sq, h + 1)
                    if h >= 2:
                        need(on_r, h - 1)
                    a = 2048 + 1024 * (h % 2)
                    mm(ps[:, a:a + TS], ones, tmp[:, h % 2, 0:TS], start=True, stop=True)
                    mm(ps[:, a + TS:a + T], ones, tmp[:, h % 2, TS + DPAD:DLEN], start=True, stop=True).then_inc(on_ss.sem, 1)

                need(mixa_ready, 2)

                def mix(k):
                    if k < 2:
                        return (mixA[:, k, 0:TS], mixA[:, k, TS + CPAD:CLEN])
                    if k < 4:
                        return (mixB[:, k - 2, 0:TS], mixB[:, k - 2, TS:T])
                    return (dnT[:, 4 + k, 0:TS], dnT[:, 4 + k, TS + DPAD:DLEN])

                for m in range(KD):
                    gg = G_OUT + m
                    s = (19 + m // 4) % 3
                    if m % 4 == 0:
                        need(ring_loaded[s], 16 * ((19 + m // 4) // 3 + 1))
                    wt = ring[s][:, 0:4096].rearrange("p (k n) -> p k n", k=KD)
                    need(gemm_out[gg % 2], gg // 2)
                    for k in range(KD):
                        if m == 0 and k >= 4:
                            need(mixc_ready, k - 3)
                        lhs = wt[:, k, (m % 4) * P:(m % 4 + 1) * P]
                        mm(gslot(gg % 2)[:, 0:TS], lhs, mix(k)[0], start=k == 0, stop=k == KD - 1)
                        ins = mm(gslot(gg % 2)[:, TS:T], lhs, mix(k)[1], start=k == 0, stop=k == KD - 1)
                    ins.then_inc(gemm_done.sem, 1)

                norm_sums(1)
                for k in range(KD):
                    need(h_ready, KD + k + 1)
                    mm(ps[0:20, 3072:3072 + TS], wr[:, k, :], hT[:, k, 0:TS], start=k == 0, stop=k == KD - 1)
                    ins = mm(ps[0:20, 3072 + TS:3072 + T], wr[:, k, :], hT[:, k, TS:T], start=k == 0, stop=k == KD - 1)
                ins.then_inc(logit_rows.sem, 1)
                need(logit_copied, 1)
                pe.sem_inc(once["pe_turns"], 1)
                for t in range(NCH):
                    ins = turn(ps[:, 2048 + 20 * t:2068 + 20 * t], lrow[:, P * t:P * (t + 1)], ident[0:20, 0:20])
                ins.then_inc(logits.sem, 1)
                need(gemm_out[0], G_MOE // 2)
                need(gemm_out[1], G_MOE // 2)
                for c_ in range(NCH):
                    if c_ >= 2:
                        need(ht_copied, c_ - 1)
                    for k in range(KD):
                        o = 1024 * (c_ % 2) + P * k
                        ins = turn(ps[:, o:o + P], hT[:, k, c_ * P:(c_ + 1) * P], ident)
                    ins.then_inc(ht_turned.sem, 1)
                need(sel_ready, 1)
                sv = rt[:, 0:80].rearrange("p (c e) -> p c e", c=NCH)
                for c_ in range(NCH):
                    for f in range(c_):
                        mm(ps[:, 3584 + NE * c_:3600 + NE * c_], ones, sv[:, f, :], start=f == 0, stop=False)
                    mm(ps[:, 3584 + NE * c_:3600 + NE * c_], cst[:, C_UP:C_UP + P], sv[:, c_, :], start=c_ == 0, stop=True)
                for f in range(NCH):
                    ins = mm(ps[:, 3664:3680], ones, sv[:, f, :], start=f == 0, stop=f == NCH - 1)
                ins.then_inc(ranks.sem, 1)

                def turn_block(q, need_b):
                    need_b(xg_loaded[q], 16, 16)
                    for k in range(KD):
                        ins = turn(ps[:, P * k:P * (k + 1)], xg[q][:, P * k:P * (k + 1)], ident)
                    ins.then_inc(xg_turned.sem, 1)

                def block(pr, q):
                    def at(n):
                        def wait(sig, base, step):
                            pe.wait_ge(sig.sem, sig.at(l, base) + (pr + n) * step)
                        return wait

                    here = at(0)
                    here(ring_loaded[q], 16 * 7 + 32, 32)
                    here(xg_copied, q + 1, 2)
                    for k in range(KD):
                        ins = mm(bank(2), xgT[q][:, k, :], ring[q][:, 512 * k:512 * k + 512], start=k == 0, stop=k == KD - 1)
                    ins.then_inc(up_done.sem, 1)
                    turn_block(1 - q, at(q))
                    here(hid_ready, q + 1, 2)
                    for f in range(FT):
                        ins = turn(bank(3)[:, P * f:P * (f + 1)], hid[:, P * f:P * (f + 1)], ident)
                    ins.then_inc(hid_turned.sem, 1)
                    here(w2_loaded[q], 16, 16)
                    here(hid_copied, q + 1, 2)
                    here(y_out, q - 1, 2)
                    for n in range(2):
                        for f in range(FT):
                            ins = mm(bank(4 + 2 * q + n), hidT[:, P * f:P * (f + 1)],
                                     ring[2][:, 2048 * q + D * f + 512 * n:2048 * q + D * f + 512 * n + 512],
                                     start=f == 0, stop=f == FT - 1)
                    ins.then_inc(y_done.sem, 1)

                need(ht_copied, NCH)
                need(slots_ready, 1)
                turn_block(0, lambda sig, base, step: need(sig, base))
                need(blocks_ready, 1)
                pe.sem_inc(once["pe_turns"], 1)
                in_use = pe.value_load(blocks[0:1, NBLK:NBLK + 1], min_val=1, max_val=NBLK)
                with pe.Fori(0, NPAIR) as pr:
                    with pe.If(pr * 2 < in_use):
                        block(pr, 0)
                        block(pr, 1)
                    with pe.Else():
                        for sig, n in ((up_done, 0), (xg_turned, 1), (hid_turned, 0), (y_done, 0)):
                            pe.wait_ge(sig.sem, sig.at(l, n) + pr * 2)
                            pe.sem_inc(sig.sem, 2)

                need(comb_done, NCH)
                need(xg_copied, NBLK + 1)
                for k in range(KD):
                    need(gemm_out[k % 2], (G_MOE + k) // 2)
                    for c_ in range(NCH):
                        ins = turn(gslot(k % 2)[:, c_ * P:(c_ + 1) * P], htok[:, c_, k * P:(k + 1) * P], ident)
                    ins.then_inc(gemm_done.sem, 1)

            for k in range(KD):
                pe.wait_ge(once["fin_sq"], k + 1)
                mm(bank(4), ones, hT[:, k, 0:TS], start=k == 0, stop=k == KD - 1)
                ins = mm(bank(5, TC), ones, hT[:, k, TS:T], start=k == 0, stop=k == KD - 1)
            ins.then_inc(once["fin_ss"], 1)
            for k in range(KD):
                pe.wait_ge(once["fin_y"], k + 1)
                if k >= 2:
                    pe.wait_ge(once["y_copied"], k - 1)
                for t in range(NCH):
                    ins = turn(gslot(k % 2)[:, t * P:(t + 1) * P], xT[:, k, t * P:(t + 1) * P], ident)
                ins.then_inc(once["y_turned"], 1)

        @block.scalar
        def _(act):
            A_ = nc.scalar.activation
            act.wait_ge(once["cst_loaded"], 16)
            act.wait_ge(once["cond_turned"], 1)
            A_(condT, bank(4, 16), ACT.Silu).then_inc(once["cond_ready"], 1)
            act.wait_ge(once["cond_ready"], 1)
            act.wait_ge(once["x_turned"], KD)
            act.wait_ge(once["pads_written"], 32)

            with act.Fori(0, L) as l:
                n_step = [0]

                def need(sig, n):
                    act.wait_ge(sig.sem, sig.at(l, n))

                def step(ins):
                    n_step[0] += 1
                    ins.then_inc(act_step.sem, 1)
                    need(act_step, n_step[0])

                need(gemm_out[0], 0)
                need(gemm_out[1], 0)
                loads = [
                    (prm[R_BMOD:R_BMOD + 48, 0, :], b_mod[l].rearrange("(r p) -> r p", p=P)),
                    (prm[R_G1:R_G1 + 8, 0, :], g1[l].rearrange("(r p) -> r p", p=P)),
                    (prm[R_G2:R_G2 + 8, 0, :], g2[l].rearrange("(r p) -> r p", p=P)),
                    (prm[R_CW:R_CW + 62, 0, :], conv_w[l].rearrange("k (r p) -> (k r) p", p=P)),
                    (prm[R_CB:R_CB + 2, 0, :], conv_b[l].rearrange("(r p) -> r p", p=P)),
                    (prm[0:2, 1, :], ln_g[l].rearrange("(r p) -> r p", p=P)),
                    (prm[2:4, 1, :], ln_b[l].rearrange("(r p) -> r p", p=P)),
                    (prm[4:64, 1, :], dn_conv_w[l].rearrange("k (r p) -> (k r) p", p=P)),
                    (prm[64:65, 1, :], norm_g[bass.ds(l, 1), :]),
                    (prm[65:73, 1, :], g_final.rearrange("(r p) -> r p", p=P)),
                    (alog, a_log[l].rearrange("(a n) -> a n", a=1).to_broadcast([P, 8])),
                    (dtb, dt_bias[l].rearrange("(a n) -> a n", a=1).to_broadcast([P, 8])),
                    (rbias[:, 0:4], bg[bass.ds(l, 1), :].to_broadcast([P, 4])),
                    (rbias[:, 4:20], be[bass.ds(l, 1), :].to_broadcast([P, 16])),
                    (wr[:, :, 0:4], wg[l].rearrange("(k p) n -> p k n", p=P)),
                    (wab, w_in[l][:, OFF_AB:PROJ].rearrange("(k p) n -> p k n", p=P)),
                    (wr[:, :, 4:20], we[l].rearrange("(k p) n -> p k n", p=P)),
                ]
                assert len(loads) == PRM_DMAS
                for dst, src in loads:
                    act.dma_start(dst, src).then_inc(prm_loaded.sem, 16)
                act.dma_start(bias_pad.ap()[:, GRID:GRID + NB],
                              rel_bias[l].rearrange("(a n) -> a n", a=1).to_broadcast([GRID, NB])).then_inc(bias_copied.sem, 16)

                def norm(n):
                    for k in range(KD):
                        A_(hT[:, k, :], xT[:, k, :], ACT.Square).then_inc(sq_ready.sem, 1)
                    need(norm_ss, n + 1)
                    step(A_(rst[:, 0:T], ps[:, 2048:2048 + T], ACT.Ln, scale=1.0 / D, bias=eps_c))
                    A_(rst[:, 0:T], rst[:, 0:T], ACT.Exp, scale=-0.5).then_inc(norm_r.sem, 1)
                    sh = 24 * n
                    for k in range(KD):
                        need(norm_x, n * KD + k + 1)
                        A_(hT[:, k, 0:TS], hT[:, k, 0:TS], ACT.Identity, scale=A[n][:, k, 0:1], bias=mod[:, sh + k, 0:1])
                        A_(hT[:, k, TS:T], hT[:, k, TS:T], ACT.Identity, scale=A[n][:, k, 1:2], bias=mod[:, sh + k, 1:2])\
                            .then_inc(h_ready.sem, 1)

                nc.scalar.preload_act_table_set("natural_log_exp_and_others")
                norm(0)
                need(bias_copied, 16)
                lo = bass.AP(tensor=bias_pad, offset=GRID + 15, ap=[[BP - 1, GRID], [CO, NH * RO], [1, GRID]])
                act.dma_start(tzv[0:GRID], lo).then_inc(bias_loaded.sem, 16)
                hi = bass.AP(tensor=bias_pad, offset=GRID + 15, ap=[[BP - 1, GRID], [CO, NH * RO - 1], [1, GRID]])
                act.dma_start(tzv[GRID:P, 1:NH * RO, :], hi).then_inc(bias_loaded.sem, 16)

                def evac(g, out, func=ACT.Copy, scale=1.0):
                    need(gemm_done, g + 1)
                    return A_(out, gslot(g % 2), func, scale=scale)

                for t in range(2):
                    evac(G_GLU + t, dnT[:, 10 + t, 0:T], scale=0.5).then_inc(gemm_out[t].sem, 1)
                for t in range(2):
                    evac(G_GLU + 2 + t, zs[:, t, :], ACT.Tanh, 0.5).then_inc(gemm_out[t].sem, 1)

                def dn_silu_of(t):
                    need(dn_conv, t + 1)
                    if t == 10:
                        need(conv_in, 2)
                    A_(dnT[:, t, 0:DLEN], tmp[:, t % 2, 0:DLEN], ACT.Silu).then_inc(dn_silu.sem, 1)

                need(pads_zeroed, 1)
                for t in range(12):
                    g = G_DN + t
                    need(gemm_done, g + 1)
                    if t >= 2:
                        need(dn_conv, t - 1)
                    A_(stage[t % 2][:, DPAD:DPAD + TS], gslot(g % 2)[:, 0:TS], ACT.Copy)
                    A_(stage[t % 2][:, 2 * DPAD + TS:2 * DPAD + T], gslot(g % 2)[:, TS:T], ACT.Copy)\
                        .then_inc(gemm_out[g % 2].sem, 1)
                    if t >= 1:
                        dn_silu_of(t - 1)
                need(conv_in, 2)
                for t in range(4):
                    evac(G_Z + t, zs[:, t, :], ACT.Silu).then_inc(gemm_out[t % 2].sem, 1)
                    if t == 0:
                        dn_silu_of(11)
                need(ab_done, 1)
                A_(ab, ps[:, 3584:3664].rearrange("p (c n) -> p c n", c=NCH), ACT.Copy).then_inc(ab_copied.sem, 1)
                need(ab_copied, 1)
                A_(beta, ab[:, :, 8:16], ACT.Tanh, scale=0.5)\
                    .then_inc(beta_tanh.sem, 1)
                for t in range(4):
                    evac(G_QK + t, qkT[:, t, :]).then_inc(gemm_out[t % 2].sem, 1)
                need(v_done, 1)
                A_(vna.rearrange("p t n -> p (t n)"), ps[:, 2048:2048 + NCH * NAW], ACT.Copy).then_inc(v_copied.sem, 1)
                for i, cache in enumerate((cache_k, cache_v)):
                    act.dma_start(kvc[i], cache[l].rearrange("s h d -> s (h d)")).then_inc(kvc_loaded.sem, 16)

                nc.scalar.preload_act_table_set("natural_log_exp_and_others")
                need(g_abs, 1)
                step(A_(gt1, gsp, ACT.Abs))
                step(A_(gt1, gt1, ACT.Exp, scale=-1.0))
                A_(gt1, gt1, ACT.Ln, bias=one_c)
                A_(ealog, alog, ACT.Exp).then_inc(g_act.sem, 1)
                need(conv_out, 1)
                for d in range(2):
                    act.dma_start(S[d], state[l, d].rearrange("h k v -> k h v")).then_inc(state_loaded.sem, 16)

                for t in range(2):
                    need(ln_xc, t + 1)
                    A_(tmp[:, t, :], mixA[:, t, :], ACT.Square).then_inc(ln_sq.sem, 1)
                need(kc_turned, 1)
                A_(kcT, ps[:, 2048:2048 + 256], ACT.Copy).then_inc(kc_copied.sem, 1)
                need(newk_turned, 1)
                A_(newk, ps[:, 2560:2560 + 256], ACT.Copy).then_inc(newk_copied.sem, 1)
                need(newk_copied, 1)
                act.dma_start(new_k[l].rearrange("s h d -> s (h d)"), newk).then_inc(newkv_stored.sem, 16)
                need(v_copied, 1)
                act.dma_start(new_v[l].rearrange("s h d -> s (h d)"), vna[:, 4, :]).then_inc(newkv_stored.sem, 16)

                need(ln_var, 1)
                step(A_(rst[:, 0:T], ps[:, 3072:3072 + T], ACT.Ln, scale=1.0 / CW, bias=eps_c))
                A_(rst[:, 0:T], rst[:, 0:T], ACT.Exp, scale=-0.5).then_inc(ln_r.sem, 1)
                for t in range(2):
                    need(ln_y, t + 1)
                    A_(mixA[:, t, :], mixA[:, t, :], ACT.Silu).then_inc(mixa_ready.sem, 1)
                nc.scalar.preload_act_table_set("natural_log_exp_and_others")

                def att_probs(i):
                    need(att_s, i + 1)
                    if i < 16:
                        A_(sc[i % 2], sc[i % 2], ACT.Exp, bias=st[:, i % 2:i % 2 + 1],
                           accum_out=st[:, 4 + i % 2:5 + i % 2]).then_inc(att_p.sem, 1)
                    else:
                        for j in range(2):
                            ins = A_(sc[i % 2][:, P * j:P * (j + 1)], sc[i % 2][:, P * j:P * (j + 1)], ACT.Exp,
                                     bias=st[:, 8 + 2 * (i % 2) + j:9 + 2 * (i % 2) + j],
                                     accum_out=st[:, 12 + 2 * (i % 2) + j:13 + 2 * (i % 2) + j])
                        ins.then_inc(att_p.sem, 1)

                def att_copy(i):
                    need(att_pt, i + 1)
                    if i >= 2:
                        need(att_o, i - 1)
                    n = T if i < 16 else 2 * P
                    A_(pT_[i % 2][:, 0:n], ps[:, 2048:2048 + n], ACT.Copy).then_inc(att_ptc.sem, 1)

                def att_store(i):
                    for h in ([i % 4] if i < 16 else [2 * (i - 16), 2 * (i - 16) + 1]):
                        u = i if i < 16 else h + 16
                        need(att_o, u + 1)
                        r = slice(64 * (h % 2), 64 * (h % 2) + 64)
                        t = slice((i // 4) * P, (i // 4 + 1) * P) if i < 16 else slice(TS, T)
                        A_(mixB[r, h // 2, t], ps[r, 512 * (6 + u % 2):512 * (6 + u % 2) + P], ACT.Copy).then_inc(att_oc.sem, 1)

                att_probs(0)
                for i in range(18):
                    if i + 1 < 18:
                        att_probs(i + 1)
                    att_copy(i)
                    if i >= 1:
                        att_store(i - 1)
                att_store(17)

                for t in range(9):
                    if t < 8:
                        if t >= 2:
                            need(l2_ss, t - 1)
                        A_(tmp[:, t % 2, 0:DLEN], dnT[:, t, 0:DLEN], ACT.Square).then_inc(l2_sq.sem, 1)
                    if t >= 1:
                        u = t - 1
                        need(l2_ss, u + 1)
                        a = 2048 + 1024 * (u % 2)
                        if u >= 1:
                            need(l2_x, u)
                        step(A_(rst[:, 0:T], ps[:, a:a + T], ACT.Ln, bias=eps_c))
                        if u < 4:
                            A_(rst[:, 0:T], rst[:, 0:T], ACT.Exp, scale=-0.5, bias=lnsc_c).then_inc(l2_r.sem, 1)
                        else:
                            A_(rst[:, 0:T], rst[:, 0:T], ACT.Exp, scale=-0.5).then_inc(l2_r.sem, 1)
                need(att_s, 18)
                for t in range(8):
                    need(kv_turned, t + 1)
                    A_(tok[:, t // 4, :, P * (t % 4):P * (t % 4 + 1)],
                       ps[:, 2048 + 1024 * (t % 2):2048 + 1024 * (t % 2) + T].rearrange("p (c n) -> p c n", c=NCH),
                       ACT.Copy).then_inc(kv_copied.sem, 1)
                need(gc_copied, 1)
                A_(egc, gcum[:, 0:40], ACT.Exp)
                A_(ekd, ekd, ACT.Exp)
                A_(cdec, gcum[:, 40:80], ACT.Exp).then_inc(gc_exp.sem, 1)

                for j in range(5):
                    for d in range(2):
                        u = 2 * j + d
                        need(dn_row, u + 1)
                        if j == 0:
                            need(newkv_stored, 32)
                        need(dn_dlog, u + 1)
                        A_(B[d]["DT"], B[d]["DT"], ACT.Exp).then_inc(dn_dexp.sem, 1)
                    for d in range(2):
                        u = 2 * j + d
                        if j:
                            need(dn_o, u - 1)
                        A_(B[d]["qdec"], heads(bank(4 * d)), ACT.Exp).then_inc(dn_erow.sem, 1)
                    for n in range(1, LEV):
                        for d in range(2):
                            need(dn_w, 2 * (LEV - 1) * j + 2 * (n - 1) + d + 1)
                            A_(B[d]["W"], heads(bank(4 * d)), ACT.Copy).then_inc(dn_wc.sem, 1)
                for d in range(2):
                    need(dn_state, 9 + d)
                    act.dma_start(new_s[l, d].rearrange("h k v -> k h v"), S[d]).then_inc(state_stored.sem, 16)

                for h in range(5):
                    if h < 4:
                        if h >= 2:
                            need(on_ss, h - 1)
                        A_(tmp[:, h % 2, 0:DLEN], dnT[:, 8 + h, 0:DLEN], ACT.Square).then_inc(on_sq.sem, 1)
                    if h >= 1:
                        u = h - 1
                        need(on_ss, u + 1)
                        if u >= 1:
                            need(mixc_ready, u)
                        a = 2048 + 1024 * (u % 2)
                        step(A_(rst[:, 0:T], ps[:, a:a + T], ACT.Ln, scale=1.0 / DK, bias=eps_c))
                        A_(rst[:, 0:T], rst[:, 0:T], ACT.Exp, scale=-0.5).then_inc(on_r.sem, 1)

                need(state_stored, 32)
                need(gemm_out[0], (G_OUT + 8) // 2)
                need(gemm_out[1], (G_OUT + 8) // 2)
                norm(1)
                need(logit_rows, 1)
                A_(lrow, ps[0:20, 3072:3072 + T], ACT.Copy).then_inc(logit_copied.sem, 1)
                need(rt_in, 1)
                A_(rt[:, 180:200], rt[:, 180:200], ACT.Exp).then_inc(rt_exp.sem, 1)
                need(rt_in2, 1)
                A_(rt[:, 350:355], rt[:, 350:355], ACT.Exp).then_inc(rt_exp2.sem, 1)
                for c_ in range(NCH):
                    need(ht_turned, c_ + 1)
                    A_(htok[:, c_, :], ps[:, 1024 * (c_ % 2):1024 * (c_ % 2) + D], ACT.Copy).then_inc(ht_copied.sem, 1)

                def wait(pr, sig, base, step):
                    act.wait_ge(sig.sem, sig.at(l, base) + pr * step)

                def copy_tokens(pr, q):
                    wait(pr, xg_turned, q + 1, 2)
                    A_(xgT[q], ps[:, 0:D].rearrange("p (k n) -> p k n", k=KD), ACT.Copy).then_inc(xg_copied.sem, 1)

                def store(pr, q):
                    wait(pr, y_out, q + 1, 2)
                    act.dma_start(ys[bass.ds((pr * 2 + q) * P, P), :], ysb[q]).then_inc(ys_stored[q].sem, 16)

                def block(pr, q):
                    wait(pr, up_done, q + 1, 2)
                    A_(sil, bank(2, FE), ACT.Silu).then_inc(sil_ready.sem, 1)
                    copy_tokens(pr + q, 1 - q)
                    wait(pr, hid_turned, q + 1, 2)
                    A_(hidT, bank(3, FE), ACT.Copy).then_inc(hid_copied.sem, 1)
                    store(pr, q)

                copy_tokens(0, 0)
                need(blocks_ready, 1)
                act.sem_inc(once["act_turns"], 1)
                in_use = act.value_load(blocks[0:1, NBLK:NBLK + 1], min_val=1, max_val=NBLK)
                with act.Fori(0, NPAIR) as pr:
                    with act.If(pr * 2 < in_use):
                        block(pr, 0)
                        block(pr, 1)
                    with act.Else():
                        for sig, n in ((sil_ready, 0), (xg_copied, 1), (hid_copied, 0)):
                            wait(pr, sig, n, 2)
                            act.sem_inc(sig.sem, 2)
                        for q in range(2):
                            wait(pr, ys_stored[q], 0, 16)
                            act.sem_inc(ys_stored[q].sem, 16)
            assert n_step[0] == ACT_STEPS, n_step
            act.wait_ge(gemm_out[0].sem, gemm_out[0].at(L, 0))
            act.wait_ge(gemm_out[1].sem, gemm_out[1].at(L, 0))
            nc.scalar.preload_act_table_set("natural_log_exp_and_others")
            for k in range(KD):
                A_(hT[:, k, :], xT[:, k, :], ACT.Square).then_inc(once["fin_sq"], 1)
            act.wait_ge(once["fin_ss"], 1)
            A_(rst[:, 0:T], ps[:, 2048:2048 + T], ACT.Ln, scale=1.0 / D, bias=eps_c).then_inc(once["fin_r"], 1)
            act.wait_ge(once["fin_r"], 1)
            A_(rst[:, 0:T], rst[:, 0:T], ACT.Exp, scale=-0.5).then_inc(once["fin_r"], 1)
            yt = xload
            for k in range(KD):
                act.wait_ge(once["y_turned"], k + 1)
                A_(yt[:, :, k * P:(k + 1) * P], gslot(k % 2).rearrange("p (c n) -> p c n", c=NCH), ACT.Copy)\
                    .then_inc(once["y_copied"], 1)
            act.wait_ge(once["y_copied"], KD)
            act.dma_start(y_sample[0].rearrange("(c p) d -> p c d", p=P), yt[:, 0:4, :]).then_inc(once["y_stored"], 16)
            act.dma_start(y_prompt[0], yt[:, 4, :]).then_inc(once["y_stored"], 16)
            act.wait_ge(newkv_stored.sem, 32 * L)
            act.wait_ge(state_stored.sem, 32 * L)
            act.wait_ge(once["y_stored"], 32)

        @block.vector
        def _(dve):
            V = nc.vector
            V.memset(zero[:, :], 0.0)
            V.memset(rst[:, 0:GRID], 0.0).then_inc(once["pad_ready"], 1)
            for k in range(KD):
                dve.wait_ge(once["pe_first"], k + 1)
                V.tensor_copy(xT[:, k, :], gslot(k % 2)).then_inc(once["x_turned"], 1)
            for s in gemm_out:
                dve.sem_inc(s.sem, 1)
            dve.sem_inc(y_out.sem, 2)
            for s in ys_stored:
                dve.sem_inc(s.sem, 16)
            dve.wait_ge(once["x_turned"], KD)
            dve.wait_ge(once["pads_written"], 32)

            with dve.Fori(0, L) as l:
                n_step = [0]

                def need(sig, n):
                    dve.wait_ge(sig.sem, sig.at(l, n))

                def count(ins):
                    n_step[0] += 1
                    ins.then_inc(dve_step.sem, 1)
                    return n_step[0]

                def step(ins):
                    need(dve_step, count(ins))

                need(gemm_done, 0)
                for s in stage:
                    V.memset(s, 0.0)
                V.memset(cin_reg[:, :], 0.0).then_inc(pads_zeroed.sem, 1)
                def mod_copy(m, bnk):
                    i = MOD_CHUNKS[m]
                    need(mod_used[i % 3], MOD_READ[i])
                    if m >= 4:
                        need(mod_turned, m - 3)
                    V.tensor_copy(mrow[m % 4], bank(bnk)[0:2]).then_inc(mod_copied.sem, 1)

                for m in range(4):
                    mod_copy(m, 4 + m % 2)
                need(prm_turned, 1)
                V.tensor_copy(pT, ps[:, 3584:3584 + 201]).then_inc(pT_ready.sem, 1)
                need(pT_ready, 1)
                need(mod_turned, 4)
                both = pT.rearrange("p (r a) -> p r a", a=1)
                step(V.tensor_tensor(mod[:, 0:16, :], ps[:, 3072:3104].rearrange("p (j c) -> p j c", c=2),
                                     both[:, 0:16].to_broadcast([P, 16, 2]), ALU.add))
                V.scalar_tensor_tensor(A[0], mod[:, 8:16, :], 1.0, both[:, R_G1:R_G1 + KD].to_broadcast([P, KD, 2]),
                                       ALU.add, ALU.mult).then_inc(mod_ready.sem, 1)

                def norm(n):
                    need(norm_r, n + 1)
                    for k in range(KD):
                        V.tensor_tensor(hT[:, k, :], xT[:, k, :], rst, ALU.mult).then_inc(norm_x.sem, 1)

                norm(0)
                need(pads_zeroed, 1)
                for t in range(2):
                    need(gemm_out[t], 2)
                    V.scalar_tensor_tensor(cin[:, t, CPAD:CPAD + TS], zs[:, t, 0:TS], 1.0, dnT[:, 10 + t, 0:TS],
                                           ALU.add, ALU.mult)
                    V.scalar_tensor_tensor(cin[:, t, 2 * CPAD + TS:2 * CPAD + T], zs[:, t, TS:T], 1.0,
                                           dnT[:, 10 + t, TS:T], ALU.add, ALU.mult).then_inc(conv_in.sem, 1)
                need(conv_in, 2)

                taps = [(k, t) for k in range(CK) for t in range(2)]
                last = [0, 0]

                def conv_tap():
                    if not taps:
                        return
                    k, t = taps.pop(0)
                    w = pT[:, R_CW + 2 * k + t:R_CW + 2 * k + t + 1]
                    src = cin[:, t, k:k + CLEN]
                    if k == 0:
                        last[t] = count(V.tensor_scalar(mixA[:, t, :], src, w, None, ALU.mult))
                    else:
                        need(dve_step, last[t])
                        last[t] = count(V.scalar_tensor_tensor(mixA[:, t, :], src, w, mixA[:, t, :], ALU.mult, ALU.add))

                for t in range(12):
                    need(gemm_out[t % 2], (G_DN + t) // 2 + 1)
                    if t >= 2:
                        need(dn_silu, t - 1)
                    out = tmp[:, t % 2, 0:DLEN]
                    for k in range(DCK):
                        w = pT[:, R_DW + 12 * k + t:R_DW + 12 * k + t + 1]
                        src = stage[t % 2][:, k:k + DLEN]
                        if k == 0:
                            n = count(V.tensor_scalar(out, src, w, None, ALU.mult))
                        else:
                            need(dve_step, n)
                            ins = V.scalar_tensor_tensor(out, src, w, out, ALU.mult, ALU.add)
                            if k == DCK - 1:
                                ins.then_inc(dn_conv.sem, 1)
                            else:
                                n = count(ins)
                        conv_tap()
                while taps:
                    conv_tap()
                need(dve_step, n_step[0])
                for t in range(2):
                    ins = V.tensor_scalar(mixA[:, t, :], mixA[:, t, :], pT[:, R_CB + t:R_CB + t + 1], None, ALU.add)
                ins.then_inc(conv_out.sem, 1)

                need(ab_copied, 1)
                row = dtb.rearrange("p (a n) -> p a n", a=1).to_broadcast([P, NCH, 8])
                V.tensor_tensor(gsp, ab[:, :, 0:8], row, ALU.add).then_inc(g_abs.sem, 1)
                need(g_act, 1)
                step(V.scalar_tensor_tensor(gsp, gsp, 0.0, gt1, ALU.max, ALU.add))
                row = ealog.rearrange("p (a n) -> p a n", a=1).to_broadcast([P, NCH, 8])
                V.scalar_tensor_tensor(gsp, gsp, -1.0, row, ALU.mult, ALU.mult)
                need(beta_tanh, 1)
                V.tensor_scalar(beta, beta, 0.5, 0.5, ALU.mult, ALU.add).then_inc(g_ready.sem, 1)

                need(conv_out, 1)
                need(ln_sum, 1)
                parts = ((slice(0, TS), slice(0, TS)), (slice(TS + CPAD, CLEN), slice(TS, T)))
                for t in range(2):
                    for a, b in parts:
                        ins = V.scalar_tensor_tensor(mixA[:, t, a], ps[:, 3072:3072 + T][:, b], -1.0 / CW, mixA[:, t, a],
                                                     ALU.mult, ALU.add)
                    ins.then_inc(ln_xc.sem, 1)
                need(ln_r, 1)
                for t in range(2):
                    for a, b in parts:
                        ins = V.scalar_tensor_tensor(mixA[:, t, a], mixA[:, t, a], pT[:, R_LNG + t:R_LNG + t + 1], rst[:, b],
                                                     ALU.mult, ALU.mult)
                    step(ins)
                    V.tensor_scalar(mixA[:, t, :], mixA[:, t, :], pT[:, R_LNB + t:R_LNB + t + 1], None, ALU.add)\
                        .then_inc(ln_y.sem, 1)

                need(tz_ready, 1)

                def att_scores(i):
                    gg = G_ATT + i
                    need(gemm_done, gg + 1)
                    if i >= 2:
                        need(att_pt, i - 1)
                    o, s = gslot(gg % 2), sc[i % 2]
                    if i < 16:
                        t, h = i // 4, i % 4
                        b = h * RO + 7 - 2 * t
                        V.scalar_tensor_tensor(s[:, 0:TS], o[:, 0:TS], HD ** -0.5, Tz[:, b * GRID:b * GRID + TS], ALU.mult, ALU.add)
                        V.tensor_scalar(s[:, TS:T], o[:, TS:T], HD ** -0.5, None, ALU.mult).then_inc(gemm_out[gg % 2].sem, 1)
                        need(gemm_out[gg % 2], gg // 2 + 1)
                        step(V.tensor_reduce(st[:, i % 2:i % 2 + 1], s, AX, ALU.max))
                        m = st[:, i % 2:i % 2 + 1]
                    else:
                        V.tensor_scalar(s[:, 0:P], o[:, 0:P], HD ** -0.5, None, ALU.mult)
                        V.tensor_scalar(s[:, P:2 * P], o[:, TS:T], HD ** -0.5, None, ALU.mult).then_inc(gemm_out[gg % 2].sem, 1)
                        need(gemm_out[gg % 2], gg // 2 + 1)
                        m = st[:, 8 + 2 * (i % 2):10 + 2 * (i % 2)]
                        step(V.tensor_reduce(m, s[:, 0:2 * P].rearrange("p (h n) -> p h n", h=2), AX, ALU.max))
                    V.tensor_scalar(m, m, -1.0, None, ALU.mult).then_inc(att_s.sem, 1)

                def att_norm(i):
                    need(att_p, i + 1)
                    s = sc[i % 2]
                    if i < 16:
                        r = st[:, 6 + i % 2:7 + i % 2]
                        step(V.reciprocal(r, st[:, 4 + i % 2:5 + i % 2]))
                        V.tensor_scalar(s, s, r, None, ALU.mult).then_inc(att_n.sem, 1)
                    else:
                        r = st[:, 12 + 2 * (i % 2):14 + 2 * (i % 2)]
                        step(V.reciprocal(r, r))
                        for j in range(2):
                            ins = V.tensor_scalar(s[:, P * j:P * (j + 1)], s[:, P * j:P * (j + 1)], r[:, j:j + 1], None, ALU.mult)
                        ins.then_inc(att_n.sem, 1)

                att_scores(0)
                for i in range(18):
                    if i + 1 < 18:
                        att_scores(i + 1)
                    att_norm(i)

                need(newkv_stored, 32)
                for t in range(9):
                    if t >= 1:
                        mod_copy(3 + t, 1)
                    if t < 8:
                        need(l2_r, t + 1)
                        V.tensor_tensor(dnT[:, t, 0:TS], dnT[:, t, 0:TS], rst[:, 0:TS], ALU.mult)
                        V.tensor_tensor(dnT[:, t, TS + DPAD:DLEN], dnT[:, t, TS + DPAD:DLEN], rst[:, TS:T], ALU.mult)\
                            .then_inc(l2_x.sem, 1)
                    if t >= 1:
                        u = t - 1
                        need(rope_mm, u + 1)
                        need(rope_cos, u + 1)
                        if u:
                            need(rope_x, u)
                        step(V.tensor_tensor(rsin, bank(2 * (u % 2)), cst[:, C_SIN:C_SIN + TS], ALU.mult))
                        V.tensor_tensor(dnT[:, u, 0:TS], rcos[u % 2], rsin, ALU.add).then_inc(rope_x.sem, 1)
                need(mod_turned, 12)
                step(V.tensor_tensor(mod[:, 16:48, :], ps[:, 1536:1600].rearrange("p (j c) -> p j c", c=2),
                                     both[:, 16:48].to_broadcast([P, 32, 2]), ALU.add))
                V.scalar_tensor_tensor(A[1], mod[:, 32:40, :], 1.0, both[:, R_G2:R_G2 + KD].to_broadcast([P, KD, 2]),
                                       ALU.add, ALU.mult).then_inc(mod2_ready.sem, 1)
                need(gc_done, 1)
                step(V.tensor_copy(gcum, ps[:, 0:80]))
                tot = gcum[:, 40:80].rearrange("p (c d h) -> p d c h", c=NCH, d=2)
                V.tensor_tensor(ekd.rearrange("p (d c h) -> p d c h", d=2, c=NCH), tot,
                                gcum[:, 0:40].rearrange("p (d c h) -> p d c h", d=2, c=NCH), ALU.subtract)\
                    .then_inc(gc_copied.sem, 1)
                need(gc_exp, 1)
                step(V.tensor_scalar(egc, egc, -1.0, None, ALU.mult))

                def chunk(j, d):
                    return 4 if j == 4 else (j if d == 0 else 3 - j)

                def col(ap, d, cc, h):
                    i = 20 * d + 4 * cc + h
                    return ap[:, i:i + 1]

                need(newkv_stored, 32)

                def decay_logs(j):
                    for d in range(2):
                        need(dn_row, 2 * j + d + 1)
                        for h in range(4):
                            ins = V.tensor_scalar(B[d]["DT"][:, h, :], bank(4 * d)[:, h * P:(h + 1) * P],
                                                  col(gcum, d, chunk(j, d), h), 0.0, ALU.subtract, ALU.min)
                        ins.then_inc(dn_dlog.sem, 1)

                decay_logs(0)
                for j in range(5):
                    for d in range(2):
                        need(dn_dexp, 2 * j + d + 1)
                        tri = cst[:, (C_UP, C_LO)[d]:(C_UP, C_LO)[d] + P]
                        masked = count(V.tensor_tensor(B[d]["DT"], B[d]["DT"], over_heads(tri), ALU.mult))
                    need(dve_step, masked)
                    for d in range(2):
                        cc = chunk(j, d)
                        need(dn_gram, 2 * j + d + 1)
                        for h in range(4):
                            ins = V.scalar_tensor_tensor(B[d]["CT"][:, h, :], bank(4 * d + 1)[:, h * P:(h + 1) * P],
                                                   beta[:, cc, 4 * d + h:4 * d + h + 1], B[d]["DT"][:, h, :], ALU.mult, ALU.mult)
                        ins.then_inc(dn_mat.sem, 1)
                    for d in range(2):
                        V.tensor_tensor(B[d]["aqk"], heads(bank(4 * d + 2)), B[d]["DT"], ALU.mult).then_inc(dn_aqk.sem, 1)
                    for d in range(2):
                        need(dn_c1, 2 * j + d + 1)
                        V.tensor_tensor(B[d]["X"], over_heads(ident), heads(bank(4 * d)), ALU.subtract)
                        V.tensor_tensor(B[d]["XT"], over_heads(ident), B[d]["Cs0"], ALU.subtract).then_inc(dn_x.sem, 1)
                    for n in range(1, LEV):
                        for d in range(2):
                            need(dn_y, 2 * (LEV - 1) * j + 2 * (n - 1) + d + 1)
                            if n < LEV - 1:
                                V.tensor_tensor(B[d]["X"], B[d]["X"], heads(bank(4 * d + 1)), ALU.subtract)
                            V.tensor_tensor(B[d]["XT"], B[d]["XT"], heads(bank(4 * d + 2)), ALU.subtract).then_inc(dn_x.sem, 1)
                    for d in range(2):
                        cc = chunk(j, d)
                        need(dn_ks, 2 * j + d + 1)
                        for h in range(4):
                            ins = V.scalar_tensor_tensor(B[d]["CT"][:, h, :], bank(4 * d + 1)[:, h * P:(h + 1) * P],
                                                         col(egc, d, cc, h), tok[:, 1, cc, h * P:(h + 1) * P], ALU.mult, ALU.add)
                        ins.then_inc(dn_res.sem, 1)
                    for d in range(2):
                        cc = chunk(j, d)
                        need(dn_u, 2 * j + d + 1)
                        V.tensor_tensor(B[d]["W"], heads(bank(4 * d + 2)), along(beta[:, cc, 4 * d:4 * d + 4], P), ALU.mult)\
                            .then_inc(dn_uu.sem, 1)
                    if j < 4:
                        decay_logs(j + 1)
                    for d in range(2):
                        cc = chunk(j, d)
                        need(dn_o, 2 * j + d + 1)
                        for h in range(4):
                            i = 8 * cc + 4 * d + h
                            V.scalar_tensor_tensor(S[d][:, h, :], S[d][:, h, :], cdec[:, i:i + 1],
                                                   bank(4 * d + 1)[:, h * P:(h + 1) * P], ALU.mult, ALU.add)
                        a = cc * P + (DPAD if cc == 4 else 0)
                        out = dnT[:, 8:12, a:a + P]
                        if (d == 0 and j in (0, 1, 4)) or (d == 1 and j < 2):
                            V.tensor_copy(out, heads(bank(4 * d + 3))).then_inc(dn_state.sem, 1)
                        else:
                            need(dn_state, 2 * j + d)
                            V.tensor_tensor(out, out, heads(bank(4 * d + 3)), ALU.add).then_inc(dn_state.sem, 1)
                    if j == 3:
                        need(dn_state, 8)
                        for d in range(2):
                            V.memset(S[d], 0.0).then_inc(ctx_zero.sem, 1)
                        need(ctx_zero, 2)

                parts = ((slice(0, TS), slice(0, TS)), (slice(TS + DPAD, DLEN), slice(TS, T)))
                for h in range(4):
                    need(on_r, h + 1)
                    for a, b in parts:
                        ins = V.scalar_tensor_tensor(dnT[:, 8 + h, a], dnT[:, 8 + h, a], pT[:, R_NG:R_NG + 1], rst[:, b],
                                                     ALU.mult, ALU.mult)
                    step(ins)
                    for a, b in parts:
                        ins = V.tensor_tensor(dnT[:, 8 + h, a], dnT[:, 8 + h, a], zs[:, h, b], ALU.mult)
                    ins.then_inc(mixc_ready.sem, 1)

                def add_to_x(m, s, gain):
                    V.scalar_tensor_tensor(xT[:, m, 0:TS], gslot(s)[:, 0:TS], mod[:, gain + m, 0:1], xT[:, m, 0:TS],
                                           ALU.mult, ALU.add)
                    V.scalar_tensor_tensor(xT[:, m, TS:T], gslot(s)[:, TS:T], mod[:, gain + m, 1:2], xT[:, m, TS:T],
                                           ALU.mult, ALU.add).then_inc(gemm_out[s].sem, 1)

                for m in range(KD):
                    need(gemm_done, G_OUT + m + 1)
                    add_to_x(m, m % 2, 16)
                norm(1)

                def r(a, n):
                    return rt[:, a:a + NCH * n].rearrange("p (c n) -> p c n", c=NCH)

                def wide(ap, n):
                    return ap.rearrange("p (c a) -> p c a", a=1).to_broadcast([P, NCH, n])

                gates, lr, e4, mx, ci, mn = r(0, 16), r(80, 20), r(180, 4), rt[:, 200:205], r(205, 4), rt[:, 225:230]
                og, psum_, ls, o1, o2 = r(230, 4), rt[:, 250:255], r(255, 4), r(275, 4), r(295, 4)
                a1, a2, w1_, l2_, dif, w2_ = rt[:, 315:320], rt[:, 320:325], rt[:, 325:330], r(330, 4), rt[:, 350:355], rt[:, 355:360]
                iota = cst[:, C_IOTA:C_IOTA + 4].rearrange("p (a n) -> p a n", a=1).to_broadcast([P, NCH, 4])

                def one_hot(out, x, best):
                    step(V.tensor_reduce(best, x, AX, ALU.max))
                    step(V.tensor_tensor(ci, x, wide(best, 4), ALU.is_equal))
                    step(V.scalar_tensor_tensor(ci, ci, -8.0, iota, ALU.mult, ALU.add))
                    step(V.tensor_reduce(mn, ci, AX, ALU.min))
                    step(V.tensor_tensor(out, ci, wide(mn, 4), ALU.is_equal))

                need(logits, 1)
                step(V.tensor_tensor(lr, ps[:, 2048:2148].rearrange("p (c n) -> p c n", c=NCH),
                                     rbias.rearrange("p (a n) -> p a n", a=1).to_broadcast([P, NCH, 20]), ALU.add))
                one_hot(og, lr[:, :, 0:4], mx)
                V.tensor_tensor(e4, lr[:, :, 0:4], wide(mx, 4), ALU.subtract).then_inc(rt_in.sem, 1)
                le = lr[:, :, 4:20].rearrange("p c (g e) -> p c g e", g=NG)
                sel = gates.rearrange("p c (g e) -> p c g e", g=NG)
                ogw = og.rearrange("p c (g a) -> p c g a", a=1).to_broadcast([P, NCH, NG, EPG])
                step(V.tensor_tensor(sel, le, ogw, ALU.mult))
                step(V.tensor_reduce(ls, gates.rearrange("p c (g e) -> p c e g", g=NG), AX, ALU.add))
                one_hot(o1, ls, a1)
                step(V.scalar_tensor_tensor(l2_, o1, NEG, ls, ALU.mult, ALU.add))
                one_hot(o2, l2_, a2)
                V.tensor_tensor(dif, a2, a1, ALU.subtract).then_inc(rt_in2.sem, 1)
                need(rt_in2, 1)

                def e16(ap):
                    return ap.rearrange("p (c g e) -> p c g e", c=NCH, g=NG)

                def spread(o):
                    return o.rearrange("p c (a e) -> p c a e", a=1).to_broadcast([P, NCH, NG, EPG])

                oh = [rsc[:, 0:80], rsc[:, 80:160]]
                V.tensor_tensor(e16(oh[0]), ogw, spread(o1), ALU.mult)
                step(V.tensor_tensor(e16(oh[1]), ogw, spread(o2), ALU.mult))
                V.tensor_tensor(rt[:, 0:80], oh[0], oh[1], ALU.add).then_inc(sel_ready.sem, 1)
                need(rt_exp, 1)
                step(V.tensor_reduce(psum_, e4, AX, ALU.add))
                step(V.reciprocal(psum_, psum_))
                need(rt_exp2, 1)
                step(V.tensor_scalar(w1_, dif, 1.0, None, ALU.add))
                step(V.reciprocal(w1_, w1_))
                step(V.tensor_tensor(w1_, w1_, psum_, ALU.mult))
                step(V.tensor_tensor(w2_, dif, w1_, ALU.mult))

                need(ranks, 1)
                nb, off, end, pos = rsc[:, 160:176], rsc[:, 176:192], rsc[:, 192:208], rsc[:, 208:288]
                pick, sl, bf, wide_ = rsc[:, 288:368], rsc[:, 368:378], rsc[:, 378:379 + NBLK], rsc[:, 410:410 + NBLK * NE]

                def last_bc(ap, n):
                    return ap.rearrange("p (e a) -> p e a", a=1).to_broadcast([P, ap.shape[-1], n])

                def mid_bc(ap, n):
                    return ap.rearrange("p (a e) -> p a e", a=1).to_broadcast([P, n, ap.shape[-1]])

                t3 = wide_[:, 0:NE * NCH].rearrange("p (e n) -> p e n", e=NE)
                step(V.tensor_tensor(t3, last_bc(ps[:, 3664:3680], NCH), mid_bc(cst[:, C_THR:C_THR + NCH], NE), ALU.is_gt))
                step(V.tensor_reduce(nb, t3, AX, ALU.add))
                step(V.tensor_scalar(nb[:, 0:1], nb[:, 0:1], 1.0, None, ALU.max))
                t3 = wide_[:, 0:NE * NE].rearrange("p (e n) -> p e n", e=NE)
                step(V.tensor_tensor(t3, mid_bc(nb, NE), cst[:, C_EXC:C_EXC + NE * NE].rearrange("p (e n) -> p e n", e=NE),
                                     ALU.mult))
                step(V.tensor_reduce(off, t3, AX, ALU.add))
                step(V.tensor_tensor(end, off, nb, ALU.add))
                step(V.tensor_scalar(off, off, float(P), -1.0, ALU.mult, ALU.add))
                c16 = pos.rearrange("p (c e) -> p c e", c=NCH)
                step(V.tensor_tensor(c16, ps[:, 3584:3664].rearrange("p (c e) -> p c e", c=NCH), mid_bc(off, NCH), ALU.add))
                for i in range(2):
                    step(V.tensor_tensor(pick, pos, oh[i], ALU.mult))
                    step(V.tensor_reduce(sl[:, NCH * i:NCH * (i + 1)], pick.rearrange("p (c e) -> p c e", c=NCH), AX, ALU.add))
                V.tensor_copy(slots[:, :], sl).then_inc(slots_ready.sem, 1)
                t3 = wide_.rearrange("p (b e) -> p b e", b=NBLK)
                step(V.tensor_tensor(t3, mid_bc(end, NBLK), last_bc(cst[:, C_BLK:C_BLK + NBLK], NE), ALU.is_le))
                step(V.tensor_reduce(bf[:, 0:NBLK], t3, AX, ALU.add))
                step(V.tensor_scalar(bf[:, 0:NBLK], bf[:, 0:NBLK], float(NE - 1), None, ALU.min))
                step(V.tensor_copy(bf[:, NBLK:NBLK + 1], end[:, NE - 1:NE]))
                V.tensor_copy(blocks[:, :], bf).then_inc(blocks_ready.sem, 1)

                def block(pr, q):
                    def wait(sig, base, step_):
                        dve.wait_ge(sig.sem, sig.at(l, base) + pr * step_)

                    wait(sil_ready, q + 1, 2)
                    V.tensor_tensor(hid, sil, bank(2)[:, FE:2 * FE], ALU.mult).then_inc(hid_ready.sem, 1)
                    wait(y_done, q + 1, 2)
                    wait(ys_stored[q], 0, 16)
                    V.tensor_copy(ysb[q], ps[:, 2048 + 1024 * q:3072 + 1024 * q]).then_inc(y_out.sem, 1)

                need(blocks_ready, 1)
                dve.sem_inc(once["dve_turns"], 1)
                in_use = dve.value_load(blocks[0:1, NBLK:NBLK + 1], min_val=1, max_val=NBLK)
                with dve.Fori(0, NPAIR) as pr:
                    with dve.If(pr * 2 < in_use):
                        block(pr, 0)
                        block(pr, 1)
                    with dve.Else():
                        for sig in (hid_ready, y_out):
                            dve.wait_ge(sig.sem, sig.at(l, 0) + pr * 2)
                            dve.sem_inc(sig.sem, 2)

                for c_ in range(NCH):
                    need(yg_loaded[c_ % 2], 32 * (c_ // 2 + 1))
                    step(V.tensor_scalar(htok[:, c_, :], yg[c_ % 2][:, 0, :], w1_[:, c_:c_ + 1], None, ALU.mult))
                    V.scalar_tensor_tensor(htok[:, c_, :], yg[c_ % 2][:, 1, :], w2_[:, c_:c_ + 1], htok[:, c_, :],
                                           ALU.mult, ALU.add).then_inc(comb_done.sem, 1)
                for k in range(KD):
                    need(gemm_done, G_MOE + k + 1)
                    add_to_x(k, k % 2, 40)

            dve.wait_ge(once["fin_r"], 2)
            for k in range(KD):
                V.scalar_tensor_tensor(xT[:, k, :], xT[:, k, :], pT[:, R_GF + k:R_GF + k + 1], rst, ALU.mult, ALU.mult)\
                    .then_inc(once["fin_y"], 1)
            assert n_step[0] == DVE_STEPS, n_step

        @block.gpsimd
        def _(pool):
            G = nc.gpsimd
            pool.wait_ge(once["cst_loaded"], 16)
            pool.wait_ge(once["pad_ready"], 1)
            pool.wait_ge(gemm_done.sem, gemm_done.at(0, G_Z))
            for rows_, nb in ((xs, NBLK + 1), (ys, NBLK)):
                for n in range(KD):
                    G.dma_start(rows_[:, n * P:(n + 1) * P].rearrange("(b p) d -> p b d", p=P),
                                zero[:, :].rearrange("p (a d) -> p a d", a=1).to_broadcast([P, nb, P])).then_inc(xys_zeroed, 16)
            with pool.Fori(0, L) as l:
                def need(sig, n):
                    pool.wait_ge(sig.sem, sig.at(l, n))

                need(bias_loaded, 32)
                table = tzv[:, 1:, :]

                def rows(a):
                    return cst[:, a:a + GRID].rearrange("p (a n) -> p a n", a=1).to_broadcast([P, NH * RO - 1, GRID])

                G.tensor_tensor(table, table, rows(C_COL), ALU.mult).then_inc(pool_step.sem, 1)
                need(pool_step, 1)
                G.tensor_tensor(table, table, rows(C_NEG), ALU.add).then_inc(tz_ready.sem, 1)

                for t in range(8):
                    need(l2_x, t + 1)
                    if t >= 2:
                        need(rope_x, t - 1)
                    G.tensor_tensor(rcos[t % 2], dnT[:, t, 0:TS], cst[:, C_COS:C_COS + TS], ALU.mult).then_inc(rope_cos.sem, 1)

                def chunk(j, d):
                    return 4 if j == 4 else (j if d == 0 else 3 - j)

                need(gc_exp, 1)
                need(kv_copied, 8)
                for j in range(5):
                    def block_of(n, d):
                        m = cst[:, C_LEV + (LEV * d + n) * P:C_LEV + (LEV * d + n + 1) * P]
                        G.tensor_tensor(B[d][f"Cs{n % 2}"], B[d]["CT"], over_heads(m), ALU.mult).then_inc(dn_cs.sem, 1)

                    for n in range(2):
                        for d in range(2):
                            need(dn_mat, 2 * j + d + 1)
                            if n == 1:
                                need(dn_aqk, 2 * j + d + 1)
                            block_of(n, d)
                    for d in range(2):
                        cc = chunk(j, d)
                        a = cc * P + (DPAD if cc == 4 else 0)
                        need(dn_erow, 2 * j + d + 1)
                        G.tensor_tensor(B[d]["qdec"], B[d]["qdec"], dnT[:, 0:4, a:a + P], ALU.mult).then_inc(dn_qk.sem, 1)
                        G.tensor_tensor(B[d]["kdec"], heads(tok[:, 0, cc, :]),
                                        along(ekd[:, 20 * d + 4 * cc:20 * d + 4 * cc + 4], P), ALU.mult).then_inc(dn_qk.sem, 1)
                    for n in range(2, LEV):
                        for d in range(2):
                            if n == 2:
                                need(dn_x, 2 * LEV * j + d + 1)
                            else:
                                need(dn_w, 2 * (LEV - 1) * j + 2 * (n - 3) + d + 1)
                            block_of(n, d)

                def settle(sig, n):
                    need(sig, n)
                    pool.sem_inc(once["pool_turns"], 1)

                need(slots_ready, 1)
                pool.wait_ge(xys_zeroed, 16 * 2 * KD)
                for c_ in range(NCH):
                    settle(ht_copied, c_ + 1)
                    for i in range(2):
                        ix = bass.IndirectOffsetOnAxis(ap=slots[:, NCH * i + c_:NCH * i + c_ + 1], axis=0)
                        G.indirect_dma_start(xs, ix, htok[:, c_, :], None).then_inc(xs_written.sem, 16)
                need(ys_stored[0], 16 * NPAIR)
                settle(ys_stored[1], 16 * NPAIR)
                for c_ in range(NCH):
                    if c_ >= 2:
                        settle(comb_done, c_ - 1)
                    for i in range(2):
                        ix = bass.IndirectOffsetOnAxis(ap=slots[:, NCH * i + c_:NCH * i + c_ + 1], axis=0)
                        G.indirect_dma_start(yg[c_ % 2][:, i, :], None, ys, ix).then_inc(yg_loaded[c_ % 2].sem, 16)


_INS = ["x_prompt", "x_sample", "cache_na_k", "cache_na_v", "state_delta", "c", "c_ctx", "w_mod", "b_mod", "g_norm1",
        "g_norm2", "w_in", "conv_a_w", "conv_a_b", "ln_a_g", "ln_a_b", "na_rel_bias", "dn_conv_w", "dn_a_log",
        "dn_dt_bias", "dn_norm_g", "w_out", "router_wg", "router_bg", "router_we", "router_be", "w1", "w3", "w2", "g_final"]
_VIEWS = {"cache_na_k": (L, P, NH, HD), "cache_na_v": (L, P, NH, HD), "state_delta": (L, 2, DH, DK, DK),
          "na_rel_bias": (L, NH * RO * CO), "dn_a_log": (L, 8), "dn_dt_bias": (L, 8)}
_OUTS = [("y_prompt", (1, TC, D)), ("y_sample", (1, TS, D)), ("new_k", (L, TC, NH, HD)), ("new_v", (L, TC, NH, HD)),
         ("new_s", (L, 2, DH, DK, DK))]


def kernel(**inputs):
    import concourse.bacc as bacc
    from concourse.bass_utils import run_bass_kernel_spmd

    nc = bacc.Bacc("TRN2", target_bir_lowering=False, num_devices=1)
    arrays, args = {}, []
    for name in [*_INS, "constants"]:
        a = constants() if name == "constants" else np.ascontiguousarray(inputs[name])
        a = a.reshape(_VIEWS.get(name, a.shape))
        arrays[f"in_{name}"] = a
        args.append(nc.dram_tensor(f"in_{name}", a.shape, F32, kind="ExternalInput").ap())
    for name, shape in _OUTS:
        args.append(nc.dram_tensor(f"out_{name}", shape, F32, kind="ExternalOutput").ap())
    build(nc, *args)
    r = run_bass_kernel_spmd(nc, [arrays], core_ids=[0])
    y_prompt, y_sample, new_k, new_v, new_s = (r.results[0][f"out_{name}"] for name, _ in _OUTS)
    return (y_prompt, y_sample, new_k.reshape(1, L, TC, NH, HD), new_v.reshape(1, L, TC, NH, HD),
            new_s.reshape(1, L, 2, DH, DK, DK))
```
